# Optimizing a Trainium2 kernel written in Bass

```python
import jax, jax.numpy as jnp
from jax import lax
import numpy as np

'''One inference step (DEPTH layers) of a hybrid autoregressive decoder.

Each layer (macaron, pre-RMSNorm, plain residual adds):
  x = x + 0.5 * SwiGLU_1(RMSNorm(x))
  x = x + Mixer(RMSNorm(x))
  x = x + 0.5 * SwiGLU_2(RMSNorm(x))
Mixer: one combined input projection -> [q, k, v, g_ret | u_pool | gate_ret, gate_pool];
  branch A: RetNet multi-scale retention (xPos-style rotation, per-head decay, chunkwise recurrent form),
            per-head RMS group norm, swish output gate -> D_MODEL wide;
  branch B: multi-scale causal pooling (4 channel groups, trailing windows 2/4/8/16, cumulative-sum form)
            minus the token, per-group linear map -> D_MODEL wide, learned per-channel scale;
  merge: sigmoid(gate_ret) * A + sigmoid(gate_pool) * B, then one output projection.
Final RMSNorm after the stack.

Inputs:
  x_prompt   (BATCH, SEQ, D_MODEL)          positions 0..SEQ-1
  x_sample   (DEC_BATCH, DEC_SEQ, D_MODEL)  positions PAST_LEN..PAST_LEN+DEC_SEQ-1
  state_ret  (DEPTH, DEC_BATCH, N_RET_HEADS, RET_QK_DIM, RET_V_DIM)  retention state after PAST_LEN tokens
  state_pool (DEPTH, DEC_BATCH, POOL_BUF, POOL_IN)                   last POOL_BUF pooling-input rows
  weights (stacked over DEPTH; norm_final shared)
Returns the tuple:
  y_prompt          (BATCH, SEQ, D_MODEL)
  y_sample          (DEC_BATCH, DEC_SEQ, D_MODEL)
  state_ret_prompt  (DEPTH, BATCH, N_RET_HEADS, RET_QK_DIM, RET_V_DIM)
  state_ret_sample  (DEPTH, DEC_BATCH, N_RET_HEADS, RET_QK_DIM, RET_V_DIM)
  state_pool_prompt (DEPTH, BATCH, POOL_BUF, POOL_IN)
  state_pool_sample (DEPTH, DEC_BATCH, POOL_BUF, POOL_IN)
'''

D_MODEL = 1024
BATCH = 1
SEQ = 256
DEPTH = 2
DEC_BATCH = 8
DEC_SEQ = 4
PAST_LEN = 2048
PAGE_SIZE = 128

N_RET_HEADS = 8
RET_QK_DIM = 64
RET_V_DIM = D_MODEL // N_RET_HEADS
RET_CHUNK = 128
ROPE_BASE = 10000.0
QK_W = N_RET_HEADS * RET_QK_DIM
V_W = N_RET_HEADS * RET_V_DIM
POOL_WINDOWS = (2, 4, 8, 16)
N_POOL_GROUPS = 4
POOL_IN = D_MODEL // 2
POOL_GROUP_IN = POOL_IN // N_POOL_GROUPS
POOL_GROUP_OUT = D_MODEL // N_POOL_GROUPS
POOL_BUF = 15
D_IN = 2 * QK_W + 2 * V_W + POOL_IN + 2 * D_MODEL
D_FF = ((8 * D_MODEL // 3 + 127) // 128) * 128
EPS = 1e-6

kernel_name = 'hybrid_retention_pool_macaron_step'

def _rmsnorm(x, g):
    xf = x.astype(jnp.float32)
    y = xf * lax.rsqrt(jnp.mean(xf * xf, axis=-1, keepdims=True) + EPS)
    return (y * g.astype(jnp.float32)).astype(x.dtype)

def _swiglu(h, w_in, w_out):
    a = h @ w_in
    gate, up = jnp.split(a, 2, axis=-1)
    return (jax.nn.silu(gate) * up) @ w_out

def _rotate(x, pos):
    half = x.shape[-1] // 2
    inv = jnp.power(jnp.float32(ROPE_BASE), -jnp.linspace(0.0, 1.0, half, dtype=jnp.float32))
    ang = pos[:, None] * inv[None, :]
    cos = jnp.cos(ang)[None, :, None, :]
    sin = jnp.sin(ang)[None, :, None, :]
    x1, x2 = x[..., :half], x[..., half:]
    return jnp.concatenate([x1 * cos - x2 * sin, x1 * sin + x2 * cos], axis=-1)

def _log_gamma():
    return jnp.log1p(-jnp.exp2(-5.0 - jnp.arange(N_RET_HEADS, dtype=jnp.float32)))

def _retention(q, k, v, s0, chunk):
    B, T, H, _ = q.shape
    n = T // chunk
    lg = _log_gamma()
    i = jnp.arange(chunk, dtype=jnp.float32)
    dist = i[:, None] - i[None, :]
    dmask = jnp.where(dist[None] >= 0, jnp.exp(lg[:, None, None] * jnp.maximum(dist, 0.0)[None]), 0.0)
    xi = jnp.exp(lg[:, None] * (i[None, :] + 1.0))
    wk = jnp.exp(lg[:, None] * (chunk - 1.0 - i[None, :]))
    g_c = jnp.exp(lg * chunk)

    def to_chunks(a):
        return a.reshape(B, n, chunk, H, a.shape[-1]).transpose(1, 0, 3, 2, 4)

    def step(s, qkv):
        qc, kc, vc = qkv
        sc = jnp.einsum('bhik,bhjk->bhij', qc, kc) * dmask[None]
        o = (jnp.einsum('bhij,bhjv->bhiv', sc, vc)
             + jnp.einsum('bhik,bhkv->bhiv', qc, s) * xi[None, :, :, None])
        s = s * g_c[None, :, None, None] + jnp.einsum('bhjk,bhjv->bhkv', kc * wk[None, :, :, None], vc)
        return s, o

    s, o = lax.scan(step, s0, (to_chunks(q), to_chunks(k), to_chunks(v)))
    o = o.transpose(1, 0, 3, 2, 4).reshape(B, T, H, v.shape[-1])
    return o, s

def _pool_branch(u, buf, pos0, w_pool, scale):
    B, T, _ = u.shape
    ext = jnp.concatenate([buf.astype(u.dtype), u], axis=1)
    cs = jnp.cumsum(ext.astype(jnp.float32), axis=1)
    cs = jnp.pad(cs, ((0, 0), (1, 0), (0, 0)))
    end = cs[:, POOL_BUF + 1:]
    pos = pos0 + jnp.arange(T, dtype=jnp.int32)
    means = []
    for g, w in enumerate(POOL_WINDOWS):
        sl = slice(g * POOL_GROUP_IN, (g + 1) * POOL_GROUP_IN)
        start = cs[:, POOL_BUF + 1 - w: POOL_BUF + 1 - w + T, sl]
        cnt = jnp.minimum(pos + 1, w).astype(jnp.float32)[None, :, None]
        means.append((end[..., sl] - start) / cnt)
    mean = jnp.concatenate(means, axis=-1)
    d = (mean - u.astype(jnp.float32)).astype(u.dtype).reshape(B, T, N_POOL_GROUPS, POOL_GROUP_IN)
    y = jnp.einsum('btgc,gcd->btgd', d, w_pool).reshape(B, T, D_MODEL) * scale
    return y, ext[:, -POOL_BUF:]

def _mixer(h, s0, buf0, pos0, chunk, w_in, w_pool, pool_scale, w_out):
    B, T, _ = h.shape
    z = h @ w_in
    idx = [QK_W, 2 * QK_W, 2 * QK_W + V_W, 2 * QK_W + 2 * V_W,
           2 * QK_W + 2 * V_W + POOL_IN, 2 * QK_W + 2 * V_W + POOL_IN + D_MODEL]
    q, k, v, g_ret, u, gate_a, gate_b = jnp.split(z, idx, axis=-1)
    pos = (pos0 + jnp.arange(T, dtype=jnp.int32)).astype(jnp.float32)
    q = _rotate(q.astype(jnp.float32).reshape(B, T, N_RET_HEADS, RET_QK_DIM), pos)
    k = _rotate(k.astype(jnp.float32).reshape(B, T, N_RET_HEADS, RET_QK_DIM), pos) * (RET_QK_DIM ** -0.5)
    v = v.astype(jnp.float32).reshape(B, T, N_RET_HEADS, RET_V_DIM)
    o, s_new = _retention(q, k, v, s0.astype(jnp.float32), chunk)
    o = o * lax.rsqrt(jnp.mean(o * o, axis=-1, keepdims=True) + EPS)
    ret = (o.reshape(B, T, V_W) * jax.nn.silu(g_ret.astype(jnp.float32))).astype(h.dtype)
    pool, buf_new = _pool_branch(u, buf0, pos0, w_pool, pool_scale)
    merged = jax.nn.sigmoid(gate_a) * ret + jax.nn.sigmoid(gate_b) * pool
    return merged @ w_out, s_new.astype(h.dtype), buf_new

def _trunk(x, ret0, pool0, pos0, chunk, norm_ffn1, w_ffn1_in, w_ffn1_out, norm_mix, w_in, w_pool,
           pool_scale, w_out, norm_ffn2, w_ffn2_in, w_ffn2_out, norm_final):
    ret_states, pool_states = [], []
    for l in range(DEPTH):
        x = x + 0.5 * _swiglu(_rmsnorm(x, norm_ffn1[l]), w_ffn1_in[l], w_ffn1_out[l])
        m, s_new, b_new = _mixer(_rmsnorm(x, norm_mix[l]), ret0[l], pool0[l], pos0, chunk,
                                 w_in[l], w_pool[l], pool_scale[l], w_out[l])
        x = x + m
        x = x + 0.5 * _swiglu(_rmsnorm(x, norm_ffn2[l]), w_ffn2_in[l], w_ffn2_out[l])
        ret_states.append(s_new)
        pool_states.append(b_new)
    return _rmsnorm(x, norm_final), jnp.stack(ret_states), jnp.stack(pool_states)

def setup_inputs(seed: int = 0) -> dict:
    key = jax.random.key(seed)
    ks = jax.random.split(key, 20)
    f32 = jnp.float32
    nrm = lambda k, shape, s: jax.random.normal(k, shape, f32) * s
    return {
        'x_prompt': nrm(ks[0], (BATCH, SEQ, D_MODEL), 1.0),
        'x_sample': nrm(ks[1], (DEC_BATCH, DEC_SEQ, D_MODEL), 1.0),
        'state_ret': nrm(ks[2], (DEPTH, DEC_BATCH, N_RET_HEADS, RET_QK_DIM, RET_V_DIM), 0.5),
        'state_pool': nrm(ks[3], (DEPTH, DEC_BATCH, POOL_BUF, POOL_IN), 1.0),
        'norm_ffn1': 1.0 + nrm(ks[4], (DEPTH, D_MODEL), 0.02),
        'w_ffn1_in': nrm(ks[5], (DEPTH, D_MODEL, 2 * D_FF), D_MODEL ** -0.5),
        'w_ffn1_out': nrm(ks[6], (DEPTH, D_FF, D_MODEL), D_FF ** -0.5),
        'norm_mix': 1.0 + nrm(ks[7], (DEPTH, D_MODEL), 0.02),
        'w_in': nrm(ks[8], (DEPTH, D_MODEL, D_IN), D_MODEL ** -0.5),
        'w_pool': nrm(ks[9], (DEPTH, N_POOL_GROUPS, POOL_GROUP_IN, POOL_GROUP_OUT), POOL_GROUP_IN ** -0.5),
        'pool_scale': 1.0 + nrm(ks[10], (DEPTH, D_MODEL), 0.02),
        'w_out': nrm(ks[11], (DEPTH, D_MODEL, D_MODEL), D_MODEL ** -0.5),
        'norm_ffn2': 1.0 + nrm(ks[12], (DEPTH, D_MODEL), 0.02),
        'w_ffn2_in': nrm(ks[13], (DEPTH, D_MODEL, 2 * D_FF), D_MODEL ** -0.5),
        'w_ffn2_out': nrm(ks[14], (DEPTH, D_FF, D_MODEL), D_FF ** -0.5),
        'norm_final': 1.0 + nrm(ks[15], (D_MODEL,), 0.02),
    }

def reference(x_prompt, x_sample, state_ret, state_pool, norm_ffn1, w_ffn1_in, w_ffn1_out, norm_mix,
              w_in, w_pool, pool_scale, w_out, norm_ffn2, w_ffn2_in, w_ffn2_out, norm_final):
    T_p = x_prompt.shape[1]
    T_s = x_sample.shape[1]
    B_p = x_prompt.shape[0]
    chunk_p = RET_CHUNK if T_p % RET_CHUNK == 0 else T_p
    ret0_p = jnp.zeros((DEPTH, B_p, N_RET_HEADS, RET_QK_DIM, RET_V_DIM), x_prompt.dtype)
    pool0_p = jnp.zeros((DEPTH, B_p, POOL_BUF, POOL_IN), x_prompt.dtype)
    y_prompt, state_ret_prompt, state_pool_prompt = _trunk(
        x_prompt, ret0_p, pool0_p, 0, chunk_p, norm_ffn1, w_ffn1_in, w_ffn1_out, norm_mix, w_in,
        w_pool, pool_scale, w_out, norm_ffn2, w_ffn2_in, w_ffn2_out, norm_final)
    y_sample, state_ret_sample, state_pool_sample = _trunk(
        x_sample, state_ret, state_pool, PAST_LEN, T_s, norm_ffn1, w_ffn1_in, w_ffn1_out, norm_mix,
        w_in, w_pool, pool_scale, w_out, norm_ffn2, w_ffn2_in, w_ffn2_out, norm_final)
    return (y_prompt, y_sample, state_ret_prompt, state_ret_sample, state_pool_prompt, state_pool_sample)


_drawn_inputs = setup_inputs


def setup_inputs(seed=0):
    import zlib

    import numpy as np

    out = dict(_drawn_inputs(seed))
    spreads = {}
    factors = {'norm_ffn1': 4.168, 'pool_scale': 21.839, 'norm_ffn2': 5.736, 'norm_final': 8.139}
    for name, (base, spread) in spreads.items():
        noise = np.random.default_rng([zlib.crc32(name.encode()), seed]).standard_normal(out[name].shape)
        drawn = base * np.exp(spread * noise) if base else spread * noise
        out[name] = __import__('jax').numpy.asarray(drawn.astype(out[name].dtype))
    for name, factor in factors.items():
        out[name] = (out[name] * factor).astype(out[name].dtype)
    return out
```

```python
from contextlib import ExitStack

import concourse.bass as bass
from concourse import mybir

F32 = mybir.dt.float32
F32R = mybir.dt.float32r
ALU = mybir.AluOpType
ACT = mybir.ActivationFunctionType

P = 128


def plan(shapes):
    class G:
        pass

    g = G()
    _, g.SEQ, g.D = shapes["x_prompt"]
    g.NB, g.NS, _ = shapes["x_sample"]
    g.L, _, g.H, g.DK, g.DV = shapes["state_ret"]
    g.BUF, g.PIN = shapes["state_pool"][2:]
    g.FF = shapes["w_ffn1_out"][1]
    g.NG = shapes["w_pool"][1]
    g.KD = g.D // P
    g.KF = g.FF // P
    g.TS = g.NB * g.NS
    g.T = g.SEQ + g.TS
    g.CH = g.SEQ // P
    g.QH = g.H // 2
    g.UK = 2 * g.KD * P
    g.UF = g.KF * P
    g.SLOT = max(g.UK, g.UF)
    g.SEG = g.BUF + g.NS
    g.PSEG = g.BUF + g.SEQ
    g.EXT = g.PSEG + g.NB * g.SEG
    g.S_F1I = 0
    g.S_F1O = g.S_F1I + g.KF
    g.S_U = g.S_F1O + g.KD
    g.S_Q = g.S_U + g.NG // 2
    g.S_WO = g.S_Q + 20
    g.S_F2I = g.S_WO + g.KD // 2
    g.S_F2O = g.S_F2I + g.KF
    g.SLOTS = g.S_F2O + g.KD
    qk, v = g.H * g.DK, g.H * g.DV
    g.C_Q, g.C_K, g.C_V, g.C_G = 0, qk, 2 * qk, 2 * qk + v
    g.C_U = 2 * qk + 2 * v
    g.C_GA = g.C_U + g.PIN
    g.C_GB = g.C_GA + g.D
    at = 0
    g.K = {}
    for name, n in (("ident", P), ("mean_d", P), ("mean_v", P), ("swap", P), ("dup0", P), ("dup1", P),
                    ("cosq", g.T), ("sinq", g.T), ("cosk", g.T), ("sink", g.T), ("inv", g.NG * 16), ("eps", 1)):
        g.K[name] = slice(at, at + n)
        at += n
    g.NK = at
    at = 0
    g.Q = {}
    for name, n in (("mask", g.QH * g.SEQ), ("smask", g.QH * g.TS), ("qmask", g.QH * g.TS),
                    ("wk", g.CH * g.QH), ("wks", g.QH * g.NB), ("decay", g.QH)):
        g.Q[name] = slice(at, at + n)
        at += n
    g.NQ = at
    assert g.SEQ == 2 * P and g.DV == P and 2 * g.DK == P and g.QH == 4 and g.NG == 4
    assert g.TS == 32 and g.KF % 2 == 0 and g.SLOTS % 2 == 0 and g.PIN == g.NG * P and g.D == g.H * g.DV
    return g


def decoder_step(nc, g, a, o):
    T, TS, SEQ, KD, KF, NB, NS, NG, QH, BUF = g.T, g.TS, g.SEQ, g.KD, g.KF, g.NB, g.NS, g.NG, g.QH, g.BUF
    ctx = ExitStack()
    with ctx:
        def sem(name):
            return ctx.enter_context(nc.semaphore(name))

        def sb(name, shape, dt=F32, stack=ctx):
            return stack.enter_context(nc.sbuf_tensor(name, shape, dt))

        raw = [sb(f"raw{p}", [P, g.SLOT]) for p in range(2)]
        whi = [sb(f"whi{p}", [P, g.SLOT], F32R) for p in range(2)]
        wlo = [sb(f"wlo{p}", [P, g.SLOT], F32R) for p in range(2)]
        x = sb("x", [P, KD, T])
        xh = sb("xh", [P, KD, T], F32R)
        xl = sb("xl", [P, KD, T], F32R)
        rb = sb("rb", [P, T])
        ssq = sb("ssq", [P, T])
        sqt = sb("sqt", [P, T])
        kc = sb("kc", [P, g.NK])
        NVEC = 4 * g.L + 1
        vecT = sb("vecT", [P, NVEC * KD])
        gl = sb("gl", [P, 5 * KD])
        over = ExitStack()
        hh = sb("hh", [P, KF, T], F32R, over)
        hl = sb("hl", [P, KF, T], F32R, over)
        fa = [sb(f"fa{p}", [P, T], F32, over) for p in range(2)]
        fs = [sb(f"fs{p}", [P, T], F32, over) for p in range(2)]
        fb = [sb(f"fb{p}", [P, T], F32, over) for p in range(2)]
        fh = [sb(f"fh{p}", [P, T], F32, over) for p in range(2)]
        over.close()
        over = ExitStack()
        tok = sb("tok", [P, g.CH + 1, g.D], F32, over)
        vrow = sb("vrow", [P, P], F32, over)
        over.close()
        mh = sb("mh", [P, KD, T], F32R)
        ml = sb("ml", [P, KD, T], F32R)
        zu = sb("zu", [P, NG, T])
        ext = sb("ext", [P, NG, g.EXT])
        dp = sb("dp", [P, NG, T])
        pq = sb("pq", [P, 4, T])
        z = sb("z", [P, 4, T])
        rot = sb("rot", [P, 4, T])
        vt = sb("vt", [P, g.CH, QH, P])
        vs = sb("vs", [TS, QH, P])
        kt = sb("kt", [P, g.CH, QH, g.DK])
        ks = sb("ks", [TS, QH, g.DK])
        ksm = [sb(f"ksm{k}", [TS, NB, g.DK]) for k in range(2)]
        sc = [sb(f"sc{h}", [P, SEQ + P]) for h in range(QH)]
        scs = [sb(f"scs{h}", [TS, TS]) for h in range(QH)]
        q2 = [sb(f"q2{h}", [P, TS]) for h in range(QH)]
        oh = sb("oh", [P, QH, T])
        over = ExitStack()
        win = [sb(f"win{k}", [P, g.EXT], F32, over) for k in range(2)]
        over.close()
        osq = [sb(f"osq{k}", [P, T]) for k in range(2)]
        rin = [sb(f"rin{k}", [P, T]) for k in range(2)]
        sg = sb("sg", [P, QH, T])
        st = sb("st", [P, NB // 2, QH, P])
        so = [sb(f"so{k}", [P, NB // 2, P]) for k in range(2)]
        sp = sb("sp", [g.DK, QH, P])
        wpq = sb("wpq", [P, 2, 2 * P])
        qc = sb("qc", [P, g.NQ])
        hist = oh[:, :, :].rearrange("p h t -> p (h t)")[0:NB * BUF, 0:g.PIN]
        PR = P - TS - BUF
        prow = z[:, :, :].rearrange("p n t -> p (n t)")[:, 0:g.PIN]

        HALF_IN = 16 * (2 + NB)
        W_STEPS = 1 + NG * (NG + 1) // 2 + 3 * NG

        def samples(row):
            return row[:, g.PSEG:g.EXT].rearrange("p (b r) -> p b r", r=g.SEG)

        big = [ctx.enter_context(nc.psum_tensor(f"acc{k}", [P, 512], F32)) for k in range(4)]
        msc = [None] * 4 + [ctx.enter_context(nc.psum_tensor(f"misc{k}", [P, 512], F32)) for k in range(4, 8)]

        ybank = [big[0], big[1], big[2], big[3], msc[6], msc[7]]

        def C(name):
            return kc[:, g.K[name]]

        def Q(name):
            return qc[:, g.Q[name]]

        START = 1

        raw_landed = [sem(f"raw_landed{p}") for p in range(2)]
        hi_done = sem("hi_done")
        lo_done = sem("lo_done")
        half_used = sem("half_used")
        const_in, x_in, vec_in, old_rows = sem("const_in"), sem("x_in"), sem("vec_in"), sem("old_rows")
        x_turned, x_start, vec_turned, vec_done, gl_done = (
            sem(n) for n in ("x_turned", "x_start", "vec_turned", "vec_done", "gl_done"))
        x_done, xh_done, xl_done = sem("x_done"), sem("xh_done"), sem("xl_done")
        sq_done, ssq_done = sem("sq_done"), sem("ssq_done")
        mean_done, rms_done, r_done = sem("mean_done"), sem("rms_done"), sem("r_done")
        gate_done, up_done, silu_done, h_done, hh_done, hl_done = (
            sem(n) for n in ("gate_done", "up_done", "silu_done", "h_done", "hh_done", "hl_done"))
        hist_in, hist_turned, hist_done, zu_done, ext_done, w_step, d_tmp, d_done = (
            sem(n) for n in ("hist_in", "hist_turned", "hist_done", "zu_done", "ext_done", "w_step", "d_tmp", "d_done"))
        pool_done, pq_done, prow_turned, prow_done, prow_out = (
            sem(n) for n in ("pool_done", "pq_done", "prow_turned", "prow_done", "prow_out"))
        half_in, z_done, swap_done, rsin_done, rcos_done, rot_done = (
            sem(n) for n in ("half_in", "z_done", "swap_done", "rsin_done", "rcos_done", "rot_done"))
        scores_done, scores_evac, v_turned, vt_done, k_turned, kt_done, ks_done, ksm_done = (
            sem(n) for n in ("scores_done", "scores_evac", "v_turned", "vt_done", "k_turned", "kt_done", "ks_done",
                             "ksm_done"))
        o_done, oh_done, osq_done, omean_done, orms_done, rin_done = (
            sem(n) for n in ("o_done", "oh_done", "osq_done", "omean_done", "orms_done", "rin_done"))
        snew_done, so_done, pnew_done, sp_done = (sem(n) for n in ("snew_done", "so_done", "pnew_done", "sp_done"))
        so_out = [sem(f"so_out{k}") for k in range(2)]
        sp_out = sem("sp_out")
        sig_done, sg_done, normed, gated_g, gated_a, gated_b, merged, mh_done, ml_done = (
            sem(n) for n in ("sig_done", "sg_done", "normed", "gated_g", "gated_a", "gated_b", "merged", "mh_done",
                             "ml_done"))
        vs_step, sc_step, kt_step = sem("vs_step"), sem("sc_step"), sem("kt_step")
        y_done, y_turned, y_evac, y_out = sem("y_done"), sem("y_turned"), sem("y_evac"), sem("y_out")

        block = ctx.enter_context(nc.Block())

        ROWS = [(c, P) for c in range(g.CH)] + [(g.CH, TS)]

        @block.sync
        def _(eng):
            for c, n in ROWS:
                src = a["x_prompt"][0, c * P:(c + 1) * P, :] if c < g.CH else a["x_sample"].rearrange("b s d -> (b s) d")
                eng.dma_start(tok[0:n, c, :], src).then_inc(x_in, 16)
            eng.dma_start(kc[:, :], a["c_all"]).then_inc(const_in, 16)
            eng.dma_start(vrow[0:NVEC * KD, :], a["c_gains"]).then_inc(vec_in, 16)
            for l in range(g.L):
                eng.dma_start(o["state_pool_sample"][l, :, 0:BUF - NS, :], a["state_pool"][l, :, NS:BUF, :])\
                   .then_inc(old_rows, 16)

            def load(l, s, p, src_a, dst_a, src_b, dst_b):
                eng.wait_ge(lo_done, 2 * (l * g.SLOTS + s) + 2)
                eng.dma_start(dst_a, src_a).then_inc(raw_landed[p], 16)
                eng.dma_start(dst_b, src_b).then_inc(raw_landed[p], 16)

            def load_two(l, s, p, w, ca, cb):
                rows = w.rearrange("(k p) c -> p k c", p=P)
                dst = raw[p][:, 0:g.UK].rearrange("p (k t c) -> p k t c", t=2, c=P)
                load(l, s, p, rows[:, :, bass.ds(ca, P)], dst[:, :, 0, :], rows[:, :, bass.ds(cb, P)], dst[:, :, 1, :])

            def load_one(l, s, p, w, c):
                rows = w.rearrange("(k p) c -> p k c", p=P)
                dst = raw[p][:, 0:g.UF].rearrange("p (k c) -> p k c", c=P)
                h = KF // 2
                load(l, s, p, rows[:, 0:h, bass.ds(c, P)], dst[:, 0:h, :], rows[:, h:KF, bass.ds(c, P)], dst[:, h:KF, :])

            def ffn(l, s0, w_in, w_out):
                with eng.Fori(0, KF // 2) as i:
                    for p in range(2):
                        load_two(l, s0 + 2 * i + p, p, w_in[l], (2 * i + p) * P, g.FF + (2 * i + p) * P)
                with eng.Fori(0, KD // 2) as i:
                    for p in range(2):
                        load_one(l, s0 + KF + 2 * i + p, p, w_out[l], (2 * i + p) * P)

            with eng.Fori(0, g.L) as l:
                ffn(l, g.S_F1I, a["w_ffn1_in"], a["w_ffn1_out"])
                w = a["w_in"][l]
                for n in range(NG // 2):
                    load_two(l, g.S_U + n, n % 2, w, g.C_U + 2 * n * P, g.C_U + (2 * n + 1) * P)
                with eng.Fori(0, 2) as i:
                    for n in range(2):
                        load_two(l, g.S_Q + 10 * i + n, n, w, g.C_Q + (2 * i + n) * P, g.C_K + (2 * i + n) * P)
                    for n, c in enumerate((g.C_V, g.C_G, g.C_GA, g.C_GB)):
                        for m in range(2):
                            col = c + (4 * i + 2 * m) * P
                            load_two(l, g.S_Q + 10 * i + 2 + 2 * n + m, m, w, col, col + P)
                with eng.Fori(0, KD // 4) as i:
                    for p in range(2):
                        load_two(l, g.S_WO + 2 * i + p, p, a["w_out"][l], (4 * i + 2 * p) * P, (4 * i + 2 * p + 1) * P)
                ffn(l, g.S_F2I, a["w_ffn2_in"], a["w_ffn2_out"])
            for c, n in ROWS:
                eng.wait_ge(y_evac, len(ROWS) + c + 1)
                dst = o["y_prompt"][0, c * P:(c + 1) * P, :] if c < g.CH else o["y_sample"].rearrange("b s d -> (b s) d")
                eng.dma_start(dst, tok[0:n, c, :]).then_inc(y_out, 16)
            eng.wait_ge(y_out, 16 * len(ROWS))
            eng.wait_ge(old_rows, 16 * g.L)
            eng.wait_ge(prow_out, START + 32 * g.L)
            for k in range(2):
                eng.wait_ge(so_out[k], START + 2 * 2 * 32 * g.L)
            eng.wait_ge(sp_out, START + 32 * g.L)

        PAIRS = g.SLOTS // 2
        HALF = g.SLOT // 2
        U_F1I, U_F1O, U_U, U_Q, U_WO, U_F2I, U_F2O = (
            n // 2 for n in (g.S_F1I, g.S_F1O, g.S_U, g.S_Q, g.S_WO, g.S_F2I, g.S_F2O))
        X_L = 3 * KD

        def number(l, u, p):
            return l * g.SLOTS + 2 * u + p

        def done(l, u, p, half=1):
            return 2 * number(l, u, p) + half + 1 + 4

        @block.tensor
        def _(eng):
            def half_slot(l, u, p, half, tiles, depth, xhi, xlo, ready):
                h = depth // 2
                eng.wait_ge(lo_done, 2 * number(l, u, p) + half + 1 + 4)
                for k in range(half * h, half * h + h):
                    ready(k)
                    for t in range(tiles):
                        at = half * HALF + ((k - half * h) * tiles + t) * P
                        w = slice(at, at + P)
                        acc = big[2 * p + t][:, 0:T]
                        eng.matmul(acc, whi[p][:, w], xhi[:, k, :], start=(k == 0), stop=False)
                        eng.matmul(acc, whi[p][:, w], xlo[:, k, :], start=False, stop=False)
                        mm = eng.matmul(acc, wlo[p][:, w], xhi[:, k, :], start=False, stop=(k == depth - 1))
                mm.then_inc(half_used, 1)

            def slot(l, u, p, tiles, depth, xhi, xlo, ready):
                for half in range(2):
                    half_slot(l, u, p, half, tiles, depth, xhi, xlo, ready)

            def x_ready(l, made):
                return lambda k: eng.wait_ge(xl_done, l * X_L + made + k + 1)

            def always(k):
                pass

            def mean(n):
                eng.wait_ge(ssq_done, 9 * n)
                eng.matmul(msc[5][:, 0:T], C("mean_d"), ssq[:, :], start=True, stop=True).then_inc(mean_done, 1)

            def ffn(l, f, u_in, u_out, made, n, free0):
                def pair(i, first):
                    for p in range(2):
                        if first:
                            eng.wait_ge(x_done, START + free0[p])
                        else:
                            eng.wait_ge(up_done, f * KF + 2 * i + p - 1)
                        slot(l, u_in + i, p, 2, KD, xh, xl, x_ready(l, made) if first and p == 0 else always)
                        if first and p == 0:
                            mean(n)

                pair(0, True)
                with eng.Fori(1, KF // 2) as i:
                    pair(i, False)

                def pair_out(i, first):
                    for p in range(2):
                        if first:
                            eng.wait_ge(up_done, f * KF + KF - 1 + p)
                        else:
                            eng.wait_ge(x_done, START + l * X_L + made + 2 * i + p - 1)

                        def h_ready(k):
                            if k in (0, KF - 2, KF - 1):
                                eng.wait_ge(hl_done, f * KF + max(k, KF - 3) + 1)
                        slot(l, u_out + i, p, 1, KF, hh, hl, h_ready if first and p == 0 else always)

                pair_out(0, True)
                with eng.Fori(1, KD // 2) as i:
                    pair_out(i, False)

            eng.sem_inc(half_used, 4)
            eng.sem_inc(snew_done, START)
            eng.wait_ge(const_in, 16)
            eng.wait_ge(vec_in, 16)
            nv = NVEC * KD
            eng.transpose(msc[7][:, 0:nv], vrow[0:nv, :], kc[0:nv, 0:nv]).then_inc(vec_turned, 1)
            eng.wait_ge(x_in, 16 * len(ROWS))
            for m in range(KD):
                if m >= 4:
                    eng.wait_ge(x_start, m - 3)
                for c, n in ROWS:
                    t = eng.transpose(big[m % 4][:, c * P:c * P + n], tok[0:n, c, m * P:(m + 1) * P], kc[0:n, 0:n])
                t.then_inc(x_turned, 1)
            eng.wait_ge(x_start, KD)

            with eng.Fori(0, g.L) as l:
                ffn(l, 2 * l, U_F1I, U_F1O, 0, 3 * l + 1, (l * X_L, l * X_L))

                for p in range(2):
                    eng.wait_ge(x_done, START + l * X_L + KD - 1 + p)
                    slot(l, U_U, p, 2, KD, xh, xl, x_ready(l, KD) if p == 0 else always)
                    if p == 0:
                        mean(3 * l + 2)
                        eng.wait_ge(hist_in, 16 * (l + 1))
                        for n in range(NG):
                            t = eng.transpose(msc[6][:, n * NB * BUF:(n + 1) * NB * BUF],
                                              hist[:, n * P:(n + 1) * P], kc[0:NB * BUF, 0:NB * BUF])
                        t.then_inc(hist_turned, 1)

                with eng.Fori(0, 2) as i:
                    half_no = 2 * l + i
                    Q4 = 4 * half_no

                    def swap(n, bank):
                        eng.matmul(bank[:, 0:T], C("swap"), z[:, n, :], start=True, stop=True).then_inc(swap_done, 1)

                    def pool(t, bank):
                        eng.matmul(bank[:, 0:T], wpq[:, t // 2, (t % 2) * P:(t % 2 + 1) * P], dp[:, 2 * i + t // 2, :],
                                   start=True, stop=True).then_inc(pool_done, 1)

                    def scores(h, bank):
                        r = slice(g.DK * (h % 2), g.DK * (h % 2 + 1))
                        q, k = rot[r, 2 * (h // 2), :], rot[r, 2 * (h // 2) + 1, :]
                        eng.matmul(bank[:, 0:SEQ], k[:, 0:P], q[:, 0:SEQ], start=True, stop=True)
                        eng.matmul(bank[:, SEQ:SEQ + P], k[:, P:SEQ], q[:, P:SEQ], start=True, stop=True)
                        eng.matmul(bank[0:TS, SEQ + P:SEQ + P + TS], k[:, SEQ:T], q[:, SEQ:T], start=True, stop=True)
                        eng.matmul(bank[:, SEQ + P + TS:SEQ + P + 2 * TS], C(f"dup{h % 2}"), rot[:, 2 * (h // 2), SEQ:T],
                                   start=True, stop=True).then_inc(scores_done, 1)

                    def turn(src, bank, s):
                        for c, n in ROWS:
                            t = eng.transpose(bank[0:n, c * P:(c + 1) * P], src[:, c * P:c * P + n], C("ident"))
                        t.then_inc(s, 1)

                    def output(h, bank):
                        eng.matmul(bank[:, 0:SEQ], vt[:, 0, h, :], sc[h][:, 0:SEQ], start=True, stop=False)
                        eng.matmul(bank[:, P:SEQ], vt[:, 1, h, :], sc[h][:, SEQ:SEQ + P], start=False, stop=True)
                        eng.matmul(bank[:, SEQ:T], vs[:, h, :], scs[h][:, :], start=True, stop=False)
                        for b in range(NB // 2):
                            w = 2 * NS
                            mm = eng.matmul(bank[:, SEQ + b * w:SEQ + (b + 1) * w], st[:, b, h, :],
                                            q2[h][:, b * w:(b + 1) * w], start=False, stop=(b == NB // 2 - 1))
                        mm.then_inc(o_done, 1)

                    def omean(h, bank):
                        eng.matmul(bank[:, 0:T], C("mean_v"), osq[h % 2][:, :], start=True, stop=True)\
                           .then_inc(omean_done, 1)

                    def state(h, bank):
                        k = ksm[h % 2][:, :, :].rearrange("t b k -> t (b k)")
                        for b in range(NB // 2):
                            mm = eng.matmul(bank[:, b * P:(b + 1) * P], k[:, b * P:(b + 1) * P], vs[:, h, :],
                                            start=True, stop=True)
                        mm.then_inc(snew_done, 1)

                    def state_prompt(bank):
                        for h in range(QH):
                            for c in range(g.CH):
                                mm = eng.matmul(bank[0:g.DK, h * P:(h + 1) * P], kt[:, c, h, :], vt[:, c, h, :],
                                                start=(c == 0), stop=(c == g.CH - 1))
                        mm.then_inc(pnew_done, 1)

                    def misc(n):
                        if n == 1:
                            eng.wait_ge(z_done, START + 5 * Q4 + 2 + 2)
                            eng.wait_ge(sp_done, START + 2 * l + i)
                            for t in range(2):
                                swap(t, msc[4 + t])
                            eng.wait_ge(half_in, HALF_IN * (2 * l + i + 1))
                            eng.wait_ge(so_done, START + Q4)
                            for t in range(2):
                                eng.wait_ge(d_done, NG * l + 2 * i + t // 2 + 1)
                                pool(t, msc[6 + t])
                        if n == 2:
                            eng.wait_ge(z_done, START + 5 * Q4 + 2 + 4)
                            for t in range(2, 4):
                                eng.wait_ge(rsin_done, Q4 + t - 1)
                                swap(t, msc[2 + t])
                            for t in range(2, 4):
                                eng.wait_ge(d_done, NG * l + 2 * i + t // 2 + 1)
                                eng.wait_ge(pq_done, Q4 + t - 1)
                                pool(t, msc[4 + t])
                        if n == 3:
                            for h in range(2):
                                eng.wait_ge(rot_done, Q4 + 2)
                                eng.wait_ge(rsin_done, Q4 + 3 + h)
                                scores(h, msc[4 + h])
                            for h in range(2):
                                eng.wait_ge(z_done, START + 5 * Q4 + 2 + 5 + h)
                                eng.wait_ge(pq_done, Q4 + 3 + h)
                                turn(z[:, h, :], msc[6 + h], v_turned)
                        if n == 4:
                            for h in range(2, 4):
                                eng.wait_ge(rot_done, Q4 + 4)
                                eng.wait_ge(scores_evac, Q4 + h - 1)
                                scores(h, msc[2 + h])
                            for h in range(2, 4):
                                eng.wait_ge(z_done, START + 5 * Q4 + 2 + 5 + h)
                                eng.wait_ge(vt_done, Q4 + h - 1)
                                turn(z[:, h, :], msc[4 + h], v_turned)
                        if n == 5:
                            for h in range(2):
                                eng.wait_ge(scores_evac, Q4 + 3 + h)
                                eng.wait_ge(vt_done, Q4 + 1 + h)
                                output(h, msc[4 + h])
                            for t in range(2):
                                eng.wait_ge(vt_done, Q4 + 3 + t)
                                turn(rot[:, 2 * t + 1, :], msc[6 + t], k_turned)
                        if n == 6:
                            for h in range(2):
                                eng.wait_ge(osq_done, Q4 + 1 + h)
                                omean(h, msc[4 + h])
                            for h in range(2, 4):
                                eng.wait_ge(kt_done, 2 * half_no + h - 1)
                                eng.wait_ge(ks_done, 2 * half_no + h - 1)
                                output(h, msc[4 + h])
                        if n == 7:
                            for h in range(2, 4):
                                eng.wait_ge(orms_done, Q4 + h - 1)
                                eng.wait_ge(osq_done, Q4 + 1 + h)
                                omean(h, msc[2 + h])
                            for h in range(2):
                                eng.wait_ge(ksm_done, Q4 + 1 + h)
                                state(h, msc[6 + h])
                        if n == 8:
                            for h in range(2, 4):
                                eng.wait_ge(ksm_done, Q4 + 1 + h)
                                eng.wait_ge(so_done, START + Q4 + h - 1)
                                state(h, msc[4 + h])
                            eng.wait_ge(orms_done, Q4 + 3)
                            state_prompt(msc[4])

                    for n in range(10):
                        p = n % 2
                        if n < 2:
                            eng.wait_ge(zu_done, NG * l + 2 * (n + 1))
                        eng.wait_ge(z_done, START + 5 * Q4 + 2 * n)
                        slot(l, U_Q + 5 * i + n // 2, p, 2, KD, xh, xl, always)
                        misc(n)

                for s in range(KD // 2):
                    if s < 2:
                        eng.wait_ge(z_done, START + 40 * (l + 1) + 2 * s)
                    else:
                        eng.wait_ge(x_done, START + l * X_L + KD + 2 * (s - 1))
                    slot(l, U_WO + s // 2, s % 2, 2, KD, mh, ml,
                         (lambda k: eng.wait_ge(ml_done, START + KD * l + k + 1)) if s == 0 else always)
                    if s == 0:
                        eng.wait_ge(sp_done, START + 2 * (l + 1))
                        for n in range(NG):
                            t = eng.transpose(msc[4][:, n * P:(n + 1) * P], zu[:, n, T - P:T], C("ident"))
                        t.then_inc(prow_turned, 1)

                ffn(l, 2 * l + 1, U_F2I, U_F2O, 2 * KD, 3 * l + 3,
                    (l * X_L + 2 * KD - 2, l * X_L + 2 * KD))

            mean(3 * g.L + 1)
            for m in range(KD):
                eng.wait_ge(y_done, m + 1)
                for c, n in ROWS:
                    t = eng.transpose(ybank[2 * c + m // 4][0:n, (m % 4) * P:(m % 4 + 1) * P],
                                      x[:, m, c * P:c * P + n], C("ident"))
                t.then_inc(y_turned, 1)

        def split_size(n):
            return {2: g.UK, 1: g.UF}[n] // 2

        def both_ends(eng, n, body):
            body(0, True, False)
            with eng.Fori(1, n - 1) as i:
                body(i, False, False)
            body(n - 1, False, True)

        def mixer_stored(eng, l):
            eng.wait_ge(prow_out, START + 32 * (l + 1))
            eng.wait_ge(sp_out, START + 32 * (l + 1))
            for k in range(2):
                eng.wait_ge(so_out[k], START + 2 * 2 * 32 * (l + 1))

        @block.scalar
        def _(eng):
            def hi(l, u, p, half, tiles):
                n = split_size(tiles)
                if half == 0:
                    eng.wait_ge(raw_landed[p], 32 * (l * PAIRS + u + 1))
                eng.wait_ge(half_used, 2 * number(l, u, p) + half + 1)
                s = slice(half * HALF, half * HALF + n)
                eng.activation(whi[p][:, s], raw[p][:, half * n:(half + 1) * n], ACT.Copy).then_inc(hi_done, 1)

            def ahead(l, u, p, tiles):
                if tiles:
                    for half in range(2):
                        hi(l, u + 1, p, half, tiles)

            def root(n):
                eng.wait_ge(mean_done, n)
                eng.wait_ge(r_done, START + n - 1)
                eng.activation(rb[:, :], msc[5][:, 0:T], ACT.Sqrt, bias=C("eps")).then_inc(rms_done, 1)

            def gained(l, made, m, gain):
                eng.wait_ge(x_done, START + l * X_L + made + m + 1)
                eng.activation(xh[:, m, :], x[:, m, :], ACT.Copy, scale=gl[:, bass.ds(gain * KD + m, 1)])\
                   .then_inc(xh_done, 1)

            def ffn(l, f, u_in, u_out, made, n, gain, after):
                def pair(i, first, last):
                    for p in range(2):
                        j = f * KF + 2 * i + p
                        ahead(l, u_in + i, p, 1 if last else 2)
                        if first and p == 0:
                            root(n)
                        eng.wait_ge(gate_done, j + 1)
                        eng.activation(fs[p][:, :], fa[p][:, :], ACT.Silu).then_inc(silu_done, 1)
                        eng.wait_ge(h_done, j + 1)
                        eng.activation(hh[:, 2 * i + p, :], fh[p][:, :], ACT.Copy).then_inc(hh_done, 1)

                both_ends(eng, KF // 2, pair)

                def pair_out(i, first, last):
                    for p in range(2):
                        ahead(l, u_out + i, p, after if last else 1)
                        gained(l, made, 2 * i + p, gain)

                both_ends(eng, KD // 2, pair_out)

            for s in (sp_done, sp_out, *so_out, prow_out):
                eng.sem_inc(s, START)
            eng.wait_ge(vec_done, 1)
            for m in range(KD):
                eng.wait_ge(x_start, m + 1)
                eng.activation(xh[:, m, :], x[:, m, :], ACT.Copy, scale=vecT[:, m:m + 1]).then_inc(xh_done, 1)

            with eng.Fori(0, g.L) as l:
                for p in range(2):
                    for half in range(2):
                        hi(l, 0, p, half, 2)
                eng.wait_ge(gl_done, l + 1)
                ffn(l, 2 * l, U_F1I, U_F1O, 0, 3 * l + 1, 1, 2)

                eng.wait_ge(ml_done, START + KD * l)
                eng.dma_start(hist, a["state_pool"][l].rearrange("b r c -> (b r) c")).then_inc(hist_in, 16)
                for p in range(2):
                    ahead(l, U_U, p, 2)
                    if p == 0:
                        root(3 * l + 2)
                        eng.wait_ge(hist_turned, l + 1)
                        for n in range(NG):
                            eng.activation(samples(ext[:, n, :])[:, :, 0:BUF],
                                           msc[6][:, n * NB * BUF:(n + 1) * NB * BUF].rearrange("p (b r) -> p b r", r=BUF),
                                           ACT.Copy).then_inc(hist_done, 1)
                    for n in range(2 * p, 2 * p + 2):
                        eng.wait_ge(zu_done, NG * l + n + 1)
                        eng.activation(ext[:, n, BUF:g.PSEG], zu[:, n, 0:SEQ], ACT.Copy).then_inc(ext_done, 1)
                        eng.activation(samples(ext[:, n, :])[:, :, BUF:g.SEG],
                                       zu[:, n, SEQ:T].rearrange("p (b s) -> p b s", s=NS), ACT.Copy).then_inc(ext_done, 1)

                with eng.Fori(0, 2) as i:
                    half_no = 2 * l + i
                    Q4 = 4 * half_no
                    eng.wait_ge(snew_done, START + Q4)
                    eng.wait_ge(so_done, START + Q4)
                    eng.dma_start(qc[:, :], a["c_half"][i]).then_inc(half_in, 16)
                    eng.dma_start(wpq[:, :, :], a["w_pool"][l, bass.ds(2 * i, 2)].rearrange("g c n -> c g n"))\
                       .then_inc(half_in, 16)
                    for b in range(NB):
                        eng.dma_start(st[(b % 2) * g.DK:(b % 2 + 1) * g.DK, b // 2, :, :],
                                      a["state_ret"][l, b, bass.ds(QH * i, QH)].rearrange("h k v -> k h v"))\
                           .then_inc(half_in, 16)

                    def pool_out(t, bank):
                        eng.wait_ge(pool_done, Q4 + t + 1)
                        if t == 0:
                            eng.wait_ge(gated_b, START + Q4)
                        eng.activation(pq[:, t, :], bank[:, 0:T], ACT.Copy, scale=gl[:, bass.ds(3 * KD + 4 * i + t, 1)])\
                           .then_inc(pq_done, 1)

                    def v_out(h, bank):
                        eng.wait_ge(v_turned, Q4 + h + 1)
                        eng.activation(vt[:, :, h, :], bank[:, 0:SEQ].rearrange("p (c v) -> p c v", v=P), ACT.Copy)\
                           .then_inc(vs_step, 1)
                        eng.activation(vs[:, h, :], bank[0:TS, SEQ:SEQ + P], ACT.Copy).then_inc(vt_done, 1)

                    def sigmoid_g(h):
                        eng.wait_ge(z_done, START + 5 * Q4 + 2 + 8 + h + 1)
                        eng.wait_ge(merged, START + Q4)
                        eng.activation(sg[:, h, :], z[:, h, :], ACT.Sigmoid).then_inc(sig_done, 1)

                    def sigmoid(n):
                        eng.wait_ge(z_done, START + 5 * Q4 + 2 + n + 1)
                        eng.activation(z[:, n % 4, :], z[:, n % 4, :], ACT.Sigmoid).then_inc(sig_done, 1)

                    def o_out(h, bank):
                        eng.wait_ge(o_done, Q4 + h + 1)
                        if h == 0:
                            eng.wait_ge(ml_done, START + Q4)
                        if h == 0:
                            eng.wait_ge(d_done, NG * (l + 1))
                        eng.activation(oh[:, h, :], bank[:, 0:T], ACT.Copy).then_inc(oh_done, 1)
                        if h >= 2:
                            eng.wait_ge(omean_done, Q4 + h - 1)
                        eng.activation(osq[h % 2][:, :], bank[:, 0:T], ACT.Square).then_inc(osq_done, 1)

                    def o_root(h, bank):
                        eng.wait_ge(omean_done, Q4 + h + 1)
                        if h >= 2:
                            eng.wait_ge(normed, Q4 + h - 1)
                        eng.activation(rin[h % 2][:, :], bank[:, 0:T], ACT.Sqrt, bias=C("eps")).then_inc(orms_done, 1)

                    def state_store(h):
                        eng.wait_ge(so_done, START + Q4 + h + 1)
                        for b2 in range(2):
                            eng.dma_start(o["state_ret_sample"][l].rearrange("(b two) h k v -> two k h b v", two=2)
                                          [b2, :, 4 * i + h], so[h % 2][b2 * g.DK:(b2 + 1) * g.DK, :, :])\
                               .then_inc(so_out[h % 2], 16)

                    def upper(h):
                        eng.wait_ge(merged, START + Q4 + h + 1)
                        eng.activation(mh[:, 4 * i + h, :], oh[:, h, :], ACT.Copy).then_inc(mh_done, 1)

                    for n in range(10):
                        ahead(l, U_Q + 5 * i + n // 2, n % 2, 2)
                        if n == 1:
                            for t in range(2):
                                pool_out(t, msc[6 + t])
                        if n == 2:
                            for t in range(2, 4):
                                pool_out(t, msc[4 + t])
                        if n == 3:
                            for h in range(2):
                                v_out(h, msc[6 + h])
                        if n == 4:
                            for h in range(2, 4):
                                v_out(h, msc[4 + h])
                            for h in range(2):
                                sigmoid_g(h)
                        if n == 5:
                            for t in range(2):
                                eng.wait_ge(kt_done, 2 * half_no + t + 1)
                                eng.activation(ks[:, 2 * t:2 * t + 2, :],
                                               msc[6 + t][0:TS, SEQ:SEQ + P].rearrange("p (h k) -> p h k", k=g.DK),
                                               ACT.Copy).then_inc(ks_done, 1)
                            for h in range(2):
                                o_out(h, msc[4 + h])
                            for h in range(2, 4):
                                sigmoid_g(h)
                        if n == 6:
                            for t in (12, 13):
                                sigmoid(t)
                            for h in range(2, 4):
                                o_out(h, msc[4 + h])
                            for h in range(2):
                                o_root(h, msc[4 + h])
                        if n == 7:
                            for h in range(2, 4):
                                o_root(h, msc[2 + h])
                            for h in range(2):
                                state_store(h)
                            for t in (14, 15):
                                sigmoid(t)
                        if n == 8:
                            for t in (16, 17):
                                sigmoid(t)
                            eng.wait_ge(pnew_done, half_no + 1)
                            eng.wait_ge(sp_out, START + 16 * half_no)
                            eng.activation(sp[:, :, :], msc[4][0:g.DK, :].rearrange("p (h v) -> p h v", v=P), ACT.Copy)\
                               .then_inc(sp_done, 1)
                            eng.wait_ge(sp_done, START + half_no + 1)
                            eng.dma_start(o["state_ret_prompt"][l, 0, bass.ds(QH * i, QH)].rearrange("h k v -> k h v"),
                                          sp[:, :, :]).then_inc(sp_out, 16)
                            for h in range(2, 4):
                                state_store(h)
                        if n == 9:
                            for h in range(2):
                                upper(h)
                            for t in (18, 19):
                                sigmoid(t)
                            for h in range(2, 4):
                                upper(h)

                for s in range(KD // 2):
                    ahead(l, U_WO + s // 2, s % 2, 2)
                    for m in range(2 * s, 2 * s + 2):
                        gained(l, KD, m, 2)
                    if s == 0:
                        eng.wait_ge(prow_turned, l + 1)
                        eng.activation(prow, msc[4][:, 0:g.PIN], ACT.Copy).then_inc(prow_done, 1)
                        eng.wait_ge(prow_done, l + 1)
                        eng.dma_start(o["state_pool_prompt"][l, 0], prow[PR:PR + BUF, :]).then_inc(prow_out, 16)
                        eng.dma_start(o["state_pool_sample"][l, :, BUF - NS:BUF, :], prow[PR + BUF:P, :]).then_inc(prow_out, 16)

                mixer_stored(eng, l)
                ffn(l, 2 * l + 1, U_F2I, U_F2O, 2 * KD, 3 * l + 3, 4, None)

            root(3 * g.L + 1)
            for e, (c, n) in enumerate([(c, n) for _ in range(2) for c, n in ROWS]):
                half = e // len(ROWS)
                eng.wait_ge(y_turned, KD // 2 * (half + 1))
                w = g.D // 2
                eng.activation(tok[0:n, c, half * w:(half + 1) * w], ybank[2 * c + half][0:n, 0:w], ACT.Copy)\
                   .then_inc(y_evac, 1)

        @block.vector
        def _(eng):
            def lo(l, u, p, half, tiles):
                n = split_size(tiles)
                eng.wait_ge(hi_done, 2 * number(l, u, p) + half + 1)
                s = slice(half * HALF, half * HALF + n)
                eng.tensor_tensor(wlo[p][:, s], raw[p][:, half * n:(half + 1) * n], whi[p][:, s].bitcast(F32), ALU.subtract).then_inc(lo_done, 1)

            def ahead(l, u, p, half, tiles):
                if tiles:
                    lo(l, u + 1, p, half, tiles)

            def invert(n):
                eng.wait_ge(rms_done, n)
                eng.reciprocal(rb[:, :], rb[:, :]).then_inc(r_done, 1)

            def lower_x(l, made, m, gain):
                eng.wait_ge(xh_done, l * X_L + KD + made + m + 1)
                eng.scalar_tensor_tensor(xl[:, m, :], x[:, m, :], gl[:, bass.ds(gain * KD + m, 1)],
                                         xh[:, m, :].bitcast(F32), ALU.mult, ALU.subtract).then_inc(xl_done, 1)

            def ffn(l, f, u_in, u_out, made, n, gain, after):
                def lower_h(j, p):
                    eng.wait_ge(hh_done, f * KF + j + 1)
                    eng.tensor_tensor(hl[:, j, :], fh[p][:, :], hh[:, j, :].bitcast(F32), ALU.subtract).then_inc(hl_done, 1)

                def pair(i, first, last):
                    for p in range(2):
                        j = 2 * i + p
                        ahead(l, u_in + i, p, 0, 1 if last else 2)
                        if first and p == 0:
                            invert(n)
                            eng.wait_ge(r_done, START + n)
                        else:
                            lower_h(j - 1, 1 - p)
                        eng.wait_ge(half_used, done(l, u_in + i, p))
                        eng.tensor_tensor(fa[p][:, :], big[2 * p][:, 0:T], rb[:, :], ALU.mult).then_inc(gate_done, 1)
                        eng.tensor_tensor(fb[p][:, :], big[2 * p + 1][:, 0:T], rb[:, :], ALU.mult).then_inc(up_done, 1)
                        ahead(l, u_in + i, p, 1, 1 if last else 2)
                        eng.wait_ge(silu_done, f * KF + j + 1)
                        eng.wait_ge(up_done, f * KF + j + 1)
                        eng.tensor_tensor(fh[p][:, :], fs[p][:, :], fb[p][:, :], ALU.mult).then_inc(h_done, 1)

                both_ends(eng, KF // 2, pair)
                lower_h(KF - 1, 1)

                def pair_out(i, first, last):
                    for p in range(2):
                        m = 2 * i + p
                        for half in range(2):
                            ahead(l, u_out + i, p, half, after if last else 1)
                        eng.wait_ge(half_used, done(l, u_out + i, p))
                        eng.scalar_tensor_tensor(x[:, m, :], big[2 * p][:, 0:T], 0.5, x[:, m, :], ALU.mult, ALU.add)\
                           .then_inc(x_done, 1)
                        lower_x(l, made, m, gain)

                both_ends(eng, KD // 2, pair_out)

            eng.sem_inc(lo_done, 4)
            eng.sem_inc(z_done, START + 2)
            for s in (x_done, r_done, so_done, ml_done):
                eng.sem_inc(s, START)
            eng.wait_ge(vec_turned, 1)
            eng.tensor_copy(vecT[:, :], msc[7][:, 0:NVEC * KD]).then_inc(vec_done, 1)
            eng.wait_ge(vec_done, 1)
            for m in range(KD):
                eng.wait_ge(x_turned, m + 1)
                eng.tensor_copy(x[:, m, :], big[m % 4][:, 0:T]).then_inc(x_start, 1)
                eng.wait_ge(xh_done, m + 1)
                eng.scalar_tensor_tensor(xl[:, m, :], x[:, m, :], vecT[:, m:m + 1], xh[:, m, :].bitcast(F32),
                                         ALU.mult, ALU.subtract).then_inc(xl_done, 1)

            with eng.Fori(0, g.L) as l:
                eng.wait_ge(xl_done, l * X_L + KD)
                eng.tensor_copy(gl[:, :], vecT[:, bass.ds(l * 4 * KD, 5 * KD)]).then_inc(gl_done, 1)
                for p in range(2):
                    for half in range(2):
                        lo(l, 0, p, half, 2)
                eng.wait_ge(gl_done, l + 1)
                ffn(l, 2 * l, U_F1I, U_F1O, 0, 3 * l + 1, 1, 2)

                for p in range(2):
                    ahead(l, U_U, p, 0, 2)
                    if p == 0:
                        invert(3 * l + 2)
                        eng.wait_ge(r_done, START + 3 * l + 2)
                    eng.wait_ge(half_used, done(l, U_U, p))
                    for t in range(2):
                        eng.tensor_tensor(zu[:, 2 * p + t, :], big[2 * p + t][:, 0:T], rb[:, :], ALU.mult)\
                           .then_inc(zu_done, 1)
                    ahead(l, U_U, p, 1, 2)

                with eng.Fori(0, 2) as i:
                    half_no = 2 * l + i
                    Q4 = 4 * half_no

                    def mask(name, h, n):
                        s = g.Q[name].start + h * n
                        return qc[:, s:s + n]

                    def cosine(n):
                        eng.wait_ge(z_done, START + 5 * Q4 + 2 + n + 1)
                        eng.tensor_tensor(rot[:, n, :], z[:, n, :], C("cosk" if n % 2 else "cosq"), ALU.mult)\
                           .then_inc(rcos_done, 1)

                    def rotate(n, bank):
                        eng.wait_ge(swap_done, Q4 + n + 1)
                        eng.wait_ge(rcos_done, Q4 + n + 1)
                        eng.tensor_tensor(z[:, n, :], bank[:, 0:T], C("sink" if n % 2 else "sinq"), ALU.mult)\
                           .then_inc(rsin_done, 1)
                        eng.wait_ge(rsin_done, Q4 + n + 1)
                        eng.tensor_tensor(rot[:, n, :], rot[:, n, :], z[:, n, :], ALU.add).then_inc(rot_done, 1)

                    def decayed(h, bank):
                        eng.wait_ge(scores_done, Q4 + h + 1)
                        m = mask("mask", h, SEQ)
                        eng.tensor_tensor(sc[h][:, 0:SEQ], bank[:, 0:SEQ], m, ALU.mult).then_inc(sc_step, 1)
                        eng.tensor_tensor(sc[h][:, SEQ:SEQ + P], bank[:, SEQ:SEQ + P], m[:, 0:P], ALU.mult).then_inc(sc_step, 1)
                        eng.tensor_tensor(scs[h][:, :], bank[0:TS, SEQ + P:SEQ + P + TS], mask("smask", h, TS)[0:TS, :],
                                          ALU.mult).then_inc(sc_step, 1)
                        eng.tensor_tensor(q2[h][:, :], bank[:, SEQ + P + TS:SEQ + P + 2 * TS], mask("qmask", h, TS),
                                          ALU.mult).then_inc(scores_evac, 1)

                    def k_out(t, bank):
                        eng.wait_ge(k_turned, 2 * half_no + t + 1)
                        wk = Q("wk").rearrange("p (c h) -> p c h", h=QH)[:, :, 2 * t:2 * t + 2]
                        for c in range(g.CH):
                            ins = eng.tensor_tensor(
                                kt[:, c, 2 * t:2 * t + 2, :],
                                bank[:, c * P:(c + 1) * P].rearrange("p (h k) -> p h k", k=g.DK),
                                wk[:, c, :].unsqueeze(2).to_broadcast([P, 2, g.DK]), ALU.mult)
                            ins.then_inc(kt_done if c == g.CH - 1 else kt_step, 1)

                    def invert_o(h):
                        eng.wait_ge(orms_done, Q4 + h + 1)
                        eng.reciprocal(rin[h % 2][:, :], rin[h % 2][:, :]).then_inc(rin_done, 1)

                    def new_state(h, bank):
                        eng.wait_ge(snew_done, START + Q4 + h + 1)
                        eng.wait_ge(so_out[h % 2], START + 32 * (2 * half_no + h // 2))
                        eng.scalar_tensor_tensor(so[h % 2][:, :, :], st[:, :, h, :], mask("decay", h, 1),
                                                 bank[:, :].rearrange("p (b v) -> p b v", v=P), ALU.mult, ALU.add)\
                           .then_inc(so_done, 1)

                    def lower(h):
                        eng.wait_ge(mh_done, Q4 + h + 1)
                        eng.tensor_tensor(ml[:, 4 * i + h, :], oh[:, h, :], mh[:, 4 * i + h, :].bitcast(F32), ALU.subtract)\
                           .then_inc(ml_done, 1)

                    def ring_free(n):
                        if n < 4:
                            eng.wait_ge(prow_out, START + 32 * l)
                            eng.wait_ge(gated_b, START + Q4)
                        elif n < 8:
                            eng.wait_ge(rot_done, Q4 + n - 3)
                        elif n < 12:
                            eng.wait_ge(v_turned, Q4 + n - 7)
                        elif n < 16:
                            eng.wait_ge(sg_done, Q4 + n - 11)
                        else:
                            eng.wait_ge(gated_a, Q4 + n - 15)

                    for n in range(10):
                        p, u = n % 2, U_Q + 5 * i + n // 2
                        ahead(l, u, p, 0, 2)
                        eng.wait_ge(half_used, done(l, u, p))
                        for t in range(2):
                            ring_free(2 * n + t)
                            eng.tensor_tensor(z[:, (2 * n + t) % 4, :], big[2 * p + t][:, 0:T], rb[:, :], ALU.mult)\
                               .then_inc(z_done, 1)
                        ahead(l, u, p, 1, 2)
                        if n < 2:
                            for t in range(2 * n, 2 * n + 2):
                                cosine(t)
                        if n == 1:
                            for t in range(2):
                                rotate(t, msc[4 + t])
                        if n == 2:
                            for t in range(2, 4):
                                rotate(t, msc[2 + t])
                        if n == 3:
                            eng.wait_ge(half_in, HALF_IN * (half_no + 1))
                            for h in range(2):
                                decayed(h, msc[4 + h])
                        if n == 4:
                            for h in range(2, 4):
                                decayed(h, msc[2 + h])
                        if n == 5:
                            for t in range(2):
                                k_out(t, msc[6 + t])
                        if n == 6:
                            for h in range(2):
                                invert_o(h)
                        if n == 7:
                            for h in range(2):
                                new_state(h, msc[6 + h])
                            for h in range(2, 4):
                                invert_o(h)
                        if n == 8:
                            for h in range(2, 4):
                                new_state(h, msc[4 + h])
                        if n == 9:
                            for h in range(4):
                                lower(h)

                for s in range(KD // 2):
                    u, p = U_WO + s // 2, s % 2
                    ahead(l, u, p, 0, 2)
                    eng.wait_ge(half_used, done(l, u, p))
                    for t in range(2):
                        eng.tensor_tensor(x[:, 2 * s + t, :], big[2 * p + t][:, 0:T], x[:, 2 * s + t, :], ALU.add)\
                           .then_inc(x_done, 1)
                    ahead(l, u, p, 1, 2)
                    for t in range(2):
                        lower_x(l, KD, 2 * s + t, 2)

                mixer_stored(eng, l)
                ffn(l, 2 * l + 1, U_F2I, U_F2O, 2 * KD, 3 * l + 3, 4, None)

            invert(3 * g.L + 1)
            eng.wait_ge(r_done, START + 3 * g.L + 1)
            for m in range(KD):
                eng.scalar_tensor_tensor(x[:, m, :], x[:, m, :], gl[:, 4 * KD + m:4 * KD + m + 1], rb[:, :],
                                         ALU.mult, ALU.mult).then_inc(y_done, 1)

        @block.gpsimd
        def _(eng):
            def squares(n, m, s, value):
                eng.wait_ge(s, value)
                eng.wait_ge(ssq_done, 9 * n + m + 1)
                eng.tensor_tensor(sqt[:, :], x[:, m, :], x[:, m, :], ALU.mult).then_inc(sq_done, 1)
                eng.wait_ge(sq_done, KD * n + m + 1)
                eng.tensor_tensor(ssq[:, :], ssq[:, :], sqt[:, :], ALU.add).then_inc(ssq_done, 1)

            def clear(n):
                if not isinstance(n, int):
                    eng.wait_ge(mean_done, n)
                eng.tensor_tensor(ssq[:, :], C("cosq"), C("cosq"), ALU.subtract).then_inc(ssq_done, 1)

            for s in (gated_b, merged):
                eng.sem_inc(s, START)
            eng.wait_ge(const_in, 16)
            clear(0)
            for m in range(KD):
                squares(0, m, x_start, m + 1)

            with eng.Fori(0, g.L) as l:
                clear(3 * l + 1)
                with eng.Fori(0, KD) as m:
                    squares(3 * l + 1, m, x_done, START + l * X_L + m + 1)

                eng.wait_ge(hist_done, NG * (l + 1))
                zero = C("cosq")[:, 0:NG * BUF].rearrange("p (n r) -> p n r", r=BUF)
                eng.tensor_tensor(ext[:, :, 0:BUF], zero, zero, ALU.subtract).then_inc(w_step, 1)
                steps = 1
                for n in range(NG):
                    eng.wait_ge(ext_done, 2 * (NG * l + n + 1))
                    src, w = ext[:, n, :], 1
                    for k in range(n + 1):
                        eng.wait_ge(w_step, W_STEPS * l + steps)
                        dst, e = win[k % 2], 2 * w - 1
                        eng.tensor_tensor(dst[:, e:g.EXT], src[:, e:g.EXT], src[:, e - w:g.EXT - w], ALU.add)\
                           .then_inc(w_step, 1)
                        steps += 1
                        src, w = dst, 2 * w
                    eng.wait_ge(w_step, W_STEPS * l + steps)
                    inv = C("inv")[:, n * 16:(n + 1) * 16]
                    eng.tensor_tensor(dp[:, n, 0:16], src[:, BUF:BUF + 16], inv, ALU.mult).then_inc(w_step, 1)
                    eng.tensor_scalar(dp[:, n, 16:SEQ], src[:, BUF + 16:g.PSEG], 1.0 / w, None, ALU.mult).then_inc(w_step, 1)
                    eng.tensor_scalar(dp[:, n, SEQ:T].rearrange("p (b s) -> p b s", s=NS),
                                      samples(src)[:, :, BUF:g.SEG], 1.0 / w, None, ALU.mult).then_inc(w_step, 1)
                    steps += 3
                    eng.wait_ge(w_step, W_STEPS * l + steps)
                    eng.tensor_tensor(dp[:, n, :], dp[:, n, :], zu[:, n, :], ALU.subtract).then_inc(d_done, 1)
                assert steps == W_STEPS

                with eng.Fori(0, 2) as i:
                    half_no = 2 * l + i
                    Q4 = 4 * half_no

                    def gated(h):
                        eng.wait_ge(sig_done, 12 * half_no + h + 1)
                        eng.tensor_tensor(sg[:, h, :], z[:, h, :], sg[:, h, :], ALU.mult).then_inc(sg_done, 1)

                    def k_masked(h):
                        eng.wait_ge(ks_done, 2 * half_no + h // 2 + 1)
                        if h >= 2:
                            eng.wait_ge(snew_done, START + Q4 + h - 1)
                        w = Q("wks").rearrange("p (h b) -> p h b", b=NB)[0:TS, h, :]
                        eng.tensor_tensor(ksm[h % 2][:, :, :], ks[:, h, :].unsqueeze(1).to_broadcast([TS, NB, g.DK]),
                                          w.unsqueeze(2).to_broadcast([TS, NB, g.DK]), ALU.mult).then_inc(ksm_done, 1)

                    def through_gates(h):
                        eng.wait_ge(rin_done, Q4 + h + 1)
                        eng.wait_ge(oh_done, Q4 + h + 1)
                        eng.tensor_tensor(oh[:, h, :], oh[:, h, :], rin[h % 2][:, :], ALU.mult).then_inc(normed, 1)
                        eng.wait_ge(normed, Q4 + h + 1)
                        eng.tensor_tensor(oh[:, h, :], oh[:, h, :], sg[:, h, :], ALU.mult).then_inc(gated_g, 1)
                        eng.wait_ge(gated_g, Q4 + h + 1)
                        eng.wait_ge(sig_done, 12 * half_no + 4 + h + 1)
                        eng.tensor_tensor(oh[:, h, :], oh[:, h, :], z[:, h, :], ALU.mult).then_inc(gated_a, 1)

                    def merge(h):
                        eng.wait_ge(sig_done, 12 * half_no + 8 + h + 1)
                        eng.wait_ge(pq_done, Q4 + h + 1)
                        eng.tensor_tensor(sg[:, h, :], pq[:, h, :], z[:, h, :], ALU.mult).then_inc(gated_b, 1)
                        eng.wait_ge(gated_b, START + Q4 + h + 1)
                        eng.wait_ge(gated_a, Q4 + h + 1)
                        eng.tensor_tensor(oh[:, h, :], oh[:, h, :], sg[:, h, :], ALU.add).then_inc(merged, 1)

                    for h in range(4):
                        gated(h)
                    eng.wait_ge(half_in, HALF_IN * (half_no + 1))
                    for h in range(2):
                        k_masked(h)
                    for h in range(2):
                        through_gates(h)
                    for h in range(2, 4):
                        k_masked(h)
                    for h in range(2, 4):
                        through_gates(h)
                    for h in range(4):
                        merge(h)

                for n, made in ((3 * l + 2, KD), (3 * l + 3, 2 * KD)):
                    clear(n)
                    with eng.Fori(0, KD) as m:
                        squares(n, m, x_done, START + l * X_L + made + m + 1)


def _constants(g):
    import numpy as np

    f = np.float32
    PAST_LEN, ROPE_BASE, EPS = 2048, 10000.0, 1e-6
    POOL_WINDOWS = (2, 4, 8, 16)
    kc = np.zeros((P, g.NK), f)

    def put(name, table):
        kc[:, g.K[name]] = table

    put("ident", np.eye(P))
    put("mean_d", 1.0 / g.D)
    put("mean_v", 1.0 / g.DV)
    half = g.DK // 2
    row = np.arange(P)
    partner = np.where(row % g.DK < half, row + half, row - half)
    put("swap", (row[:, None] == partner[None, :]).astype(f))
    for par in range(2):
        put(f"dup{par}", (row[:, None] == par * g.DK + row[None, :] % g.DK).astype(f))
    pos = np.concatenate([np.arange(g.SEQ), np.tile(PAST_LEN + np.arange(g.NS), g.NB)]).astype(f)
    inv = np.power(f(ROPE_BASE), -np.linspace(0.0, 1.0, half, dtype=f)).astype(f)
    ang = (pos[None, :] * inv[row % half][:, None]).astype(f)
    sign = np.where(row % g.DK < half, -1.0, 1.0).astype(f)[:, None]
    cos, sin = np.cos(ang), np.sin(ang) * sign
    put("cosq", cos)
    put("sinq", sin)
    put("cosk", cos * f(g.DK ** -0.5))
    put("sink", sin * f(g.DK ** -0.5))
    t = np.arange(16)
    put("inv", np.concatenate([1.0 / np.minimum(t + 1, w) for w in POOL_WINDOWS])[None, :])
    put("eps", EPS)

    lg = np.log1p(-np.exp2(-5.0 - np.arange(g.H, dtype=np.float64)))
    qc = np.zeros((2, P, g.NQ), f)
    j, i = np.arange(P), np.arange(g.SEQ)
    tok = np.arange(g.TS)
    b, s = tok // g.NS, tok % g.NS
    for h in range(g.H):
        half_no, hh = divmod(h, g.QH)

        def half_put(name, n, table, rows=P):
            at = g.Q[name].start + hh * n
            qc[half_no, 0:rows, at:at + n] = table

        dist = i[None, :] - j[:, None]
        half_put("mask", g.SEQ, np.where(dist >= 0, np.exp(lg[h] * np.maximum(dist, 0)), 0.0))
        dist = s[None, :] - s[:, None]
        same = b[None, :] == b[:, None]
        half_put("smask", g.TS, np.where(same & (dist >= 0), np.exp(lg[h] * np.maximum(dist, 0)), 0.0), g.TS)
        half_put("qmask", g.TS, np.where(b[None, :] % 2 == (row // g.DK)[:, None], np.exp(lg[h] * (s + 1.0))[None, :], 0.0))
        half_put("wks", g.NB, np.where(b[:, None] == np.arange(g.NB)[None, :], np.exp(lg[h] * (g.NS - 1.0 - s))[:, None], 0.0), g.TS)
        half_put("decay", 1, np.exp(lg[h] * g.NS))
        for c in range(g.CH):
            qc[half_no, :, g.Q["wk"].start + c * g.QH + hh] = np.exp(lg[h] * (g.SEQ - 1.0 - (c * P + j)))
    return kc, qc


def kernel(**inputs):
    import numpy as np
    import concourse.bacc as bacc
    from concourse.bass_utils import run_bass_kernel_spmd

    nc = bacc.Bacc("TRN2", target_bir_lowering=False, num_devices=1)
    g = plan({n: v.shape for n, v in inputs.items()})
    kc, qc = _constants(g)
    arrays = {n: np.ascontiguousarray(inputs[n]) for n in (
        "x_prompt", "x_sample", "state_ret", "state_pool", "w_ffn1_in", "w_ffn1_out", "w_in", "w_pool", "w_out",
        "w_ffn2_in", "w_ffn2_out")}
    rows = [np.asarray(inputs[n])[l] for l in range(g.L) for n in ("norm_ffn1", "norm_mix", "norm_ffn2", "pool_scale")]
    arrays["c_gains"] = np.ascontiguousarray(np.stack(rows + [np.asarray(inputs["norm_final"])]).reshape(-1, P))
    arrays["c_all"], arrays["c_half"] = kc, qc
    outs = {
        "y_prompt": (1, g.SEQ, g.D), "y_sample": (g.NB, g.NS, g.D),
        "state_ret_prompt": (g.L, 1, g.H, g.DK, g.DV), "state_ret_sample": (g.L, g.NB, g.H, g.DK, g.DV),
        "state_pool_prompt": (g.L, 1, g.BUF, g.PIN), "state_pool_sample": (g.L, g.NB, g.BUF, g.PIN),
    }
    a = {n: nc.dram_tensor("in_" + n, v.shape, F32, kind="ExternalInput").ap() for n, v in arrays.items()}
    o = {n: nc.dram_tensor("out_" + n, s, F32, kind="ExternalOutput").ap() for n, s in outs.items()}
    decoder_step(nc, g, a, o)
    r = run_bass_kernel_spmd(nc, [{"in_" + n: v for n, v in arrays.items()}], core_ids=[0])
    return tuple(r.results[0]["out_" + n] for n in outs)
```

```python
from contextlib import ExitStack

import concourse.bass as bass
from concourse import mybir

F32 = mybir.dt.float32
F32R = mybir.dt.float32r
ALU = mybir.AluOpType
ACT = mybir.ActivationFunctionType

P = 128


def plan(shapes):
    class G:
        pass

    g = G()
    _, g.SEQ, g.D = shapes["x_prompt"]
    g.NB, g.NS, _ = shapes["x_sample"]
    g.L, _, g.H, g.DK, g.DV = shapes["state_ret"]
    g.BUF, g.PIN = shapes["state_pool"][2:]
    g.FF = shapes["w_ffn1_out"][1]
    g.NG = shapes["w_pool"][1]
    g.KD = g.D // P
    g.KF = g.FF // P
    g.TS = g.NB * g.NS
    g.T = g.SEQ + g.TS
    g.CH = g.SEQ // P
    g.QH = g.H // 2
    g.UK = 2 * g.KD * P
    g.UF = g.KF * P
    g.SLOT = max(g.UK, g.UF)
    g.SEG = g.BUF + g.NS
    g.PSEG = g.BUF + g.SEQ
    g.EXT = g.PSEG + g.NB * g.SEG
    g.S_F1I = 0
    g.S_F1O = g.S_F1I + g.KF
    g.S_U = g.S_F1O + g.KD
    g.S_Q = g.S_U + g.NG // 2
    g.S_WO = g.S_Q + 20
    g.S_F2I = g.S_WO + g.KD // 2
    g.S_F2O = g.S_F2I + g.KF
    g.SLOTS = g.S_F2O + g.KD
    qk, v = g.H * g.DK, g.H * g.DV
    g.C_Q, g.C_K, g.C_V, g.C_G = 0, qk, 2 * qk, 2 * qk + v
    g.C_U = 2 * qk + 2 * v
    g.C_GA = g.C_U + g.PIN
    g.C_GB = g.C_GA + g.D
    at = 0
    g.K = {}
    for name, n in (("ident", P), ("mean_d", P), ("mean_v", P), ("dup0", P), ("dup1", P),
                    ("cosq", g.T), ("sinq", g.T), ("cosk", g.T), ("sink", g.T), ("inv", g.NG * 16), ("eps", 1)):
        g.K[name] = slice(at, at + n)
        at += n
    g.NK = at
    at = 0
    g.Q = {}
    for name, n in (("mask", g.QH * g.SEQ), ("smask", g.QH * g.TS), ("qmask", g.QH * g.TS),
                    ("wk", g.CH * g.QH), ("wks", g.QH * g.NB), ("decay", g.QH)):
        g.Q[name] = slice(at, at + n)
        at += n
    g.NQ = at
    assert g.SEQ == 2 * P and g.DV == P and 2 * g.DK == P and g.QH == 4 and g.NG == 4
    assert g.TS == 32 and g.KF % 2 == 0 and g.SLOTS % 2 == 0 and g.PIN == g.NG * P and g.D == g.H * g.DV
    return g


def decoder_step(nc, g, a, o):
    T, TS, SEQ, KD, KF, NB, NS, NG, QH, BUF = g.T, g.TS, g.SEQ, g.KD, g.KF, g.NB, g.NS, g.NG, g.QH, g.BUF
    ctx = ExitStack()
    with ctx:
        def sem(name):
            return ctx.enter_context(nc.semaphore(name))

        def sb(name, shape, dt=F32, stack=ctx):
            return stack.enter_context(nc.sbuf_tensor(name, shape, dt))

        raw = [sb(f"raw{p}", [P, g.SLOT]) for p in range(2)]
        whi = [sb(f"whi{p}", [P, g.SLOT], F32R) for p in range(2)]
        wlo = [sb(f"wlo{p}", [P, g.SLOT], F32R) for p in range(2)]
        x = sb("x", [P, KD, T])
        xh = sb("xh", [P, KD, T], F32R)
        xl = sb("xl", [P, KD, T], F32R)
        rb = sb("rb", [P, T])
        ssq = sb("ssq", [P, T])
        sqt = sb("sqt", [P, T])
        kc = sb("kc", [P, g.NK])
        identr = sb("identr", [P, P], F32R)
        rcol = sb("rcol", [P, g.CH + 1])
        NVEC = 4 * g.L + 1
        vecT = sb("vecT", [P, NVEC * KD])
        gl = sb("gl", [P, 5 * KD])
        over = ExitStack()
        hh = sb("hh", [P, KF, T], F32R, over)
        hl = sb("hl", [P, KF, T], F32R, over)
        fa = [sb(f"fa{p}", [P, T], F32, over) for p in range(2)]
        fs = [sb(f"fs{p}", [P, T], F32, over) for p in range(2)]
        fh = [sb(f"fh{p}", [P, T], F32, over) for p in range(2)]
        over.close()
        over = ExitStack()
        tok = sb("tok", [P, g.CH + 1, g.D], F32, over)
        vrow = sb("vrow", [P, P], F32, over)
        over.close()
        mh = sb("mh", [P, KD, T], F32R)
        ml = sb("ml", [P, KD, T], F32R)
        zu = sb("zu", [P, NG, T])
        ext = sb("ext", [P, NG, g.EXT])
        dp = sb("dp", [P, NG, T])
        pq = sb("pq", [P, 4, T])
        z = sb("z", [P, 4, T])
        rot = sb("rot", [P, 4, T])
        vt = sb("vt", [P, g.CH, QH, P])
        vs = sb("vs", [TS, QH, P])
        kt = sb("kt", [P, g.CH, QH, g.DK])
        ks = sb("ks", [TS, QH, g.DK])
        ksm = [sb(f"ksm{k}", [TS, NB, g.DK]) for k in range(2)]
        sc = [sb(f"sc{h}", [P, SEQ + P]) for h in range(QH)]
        scs = [sb(f"scs{h}", [TS, TS]) for h in range(QH)]
        q2 = [sb(f"q2{h}", [P, TS]) for h in range(QH)]
        oh = sb("oh", [P, QH, T])
        over = ExitStack()
        win = [sb(f"win{k}", [P, g.EXT], F32, over) for k in range(2)]
        over.close()
        osq = [sb(f"osq{k}", [P, T]) for k in range(2)]
        rin = [sb(f"rin{k}", [P, T]) for k in range(2)]
        sg = sb("sg", [P, QH, T])
        st = sb("st", [P, NB // 2, QH, P])
        so = [sb(f"so{k}", [P, NB // 2, P]) for k in range(2)]
        sp = sb("sp", [g.DK, QH, P])
        wpq = sb("wpq", [P, 2, 2 * P])
        qc = sb("qc", [P, g.NQ])
        hist = oh[:, :, :].rearrange("p h t -> p (h t)")[0:NB * BUF, 0:g.PIN]
        PR = P - TS - BUF
        prow = z[:, :, :].rearrange("p n t -> p (n t)")[:, 0:g.PIN]

        HALF_IN = 32
        W_STEPS = 1 + NG * (NG + 1) // 2 + 3 * NG

        def samples(row):
            return row[:, g.PSEG:g.EXT].rearrange("p (b r) -> p b r", r=g.SEG)

        big = [ctx.enter_context(nc.psum_tensor(f"acc{k}", [P, 512], F32)) for k in range(4)]
        msc = [None] * 4 + [ctx.enter_context(nc.psum_tensor(f"misc{k}", [P, 512], F32)) for k in range(4, 8)]

        ybank = [big[0], big[1], big[2], big[3], msc[6], msc[7]]

        def C(name):
            return kc[:, g.K[name]]

        def Q(name):
            return qc[:, g.Q[name]]

        START = 1

        raw_landed = [sem(f"raw_landed{p}") for p in range(2)]
        hi_done = sem("hi_done")
        lo_done = sem("lo_done")
        half_used = sem("half_used")
        ident_in, const_in, x_in, vec_in, old_rows = (
            sem(n) for n in ("ident_in", "const_in", "x_in", "vec_in", "old_rows"))
        identr_done = sem("identr_done")
        x_turned, x_start, vec_turned, vec_done, gl_done = (
            sem(n) for n in ("x_turned", "x_start", "vec_turned", "vec_done", "gl_done"))
        x_done, xh_done, xl_done = sem("x_done"), sem("xh_done"), sem("xl_done")
        sq_done, ssq_done = sem("sq_done"), sem("ssq_done")
        mean_done, rms_done, r_done = sem("mean_done"), sem("rms_done"), sem("r_done")
        gate_done, scaled_done, silu_done, h_done, hh_done, hl_done = (
            sem(n) for n in ("gate_done", "scaled_done", "silu_done", "h_done", "hh_done", "hl_done"))
        hist_in, hist_turned, hist_done, zu_done, ext_done, w_step, d_tmp, d_done = (
            sem(n) for n in ("hist_in", "hist_turned", "hist_done", "zu_done", "ext_done", "w_step", "d_tmp", "d_done"))
        pool_done, pq_done, prow_turned, prow_done, prow_out = (
            sem(n) for n in ("pool_done", "pq_done", "prow_turned", "prow_done", "prow_out"))
        half_in, states_in, z_done, swap_done, rsin_done, rsum_done, rot_done = (
            sem(n) for n in ("half_in", "states_in", "z_done", "swap_done", "rsin_done", "rsum_done", "rot_done"))
        scores_done, scores_evac, v_turned, vt_done, k_turned, kt_done, ks_done, ksm_done = (
            sem(n) for n in ("scores_done", "scores_evac", "v_turned", "vt_done", "k_turned", "kt_done", "ks_done",
                             "ksm_done"))
        o_done, oh_done, osq_done, omean_done, orms_done, rin_done = (
            sem(n) for n in ("o_done", "oh_done", "osq_done", "omean_done", "orms_done", "rin_done"))
        snew_done, so_done, pnew_done, sp_done = (sem(n) for n in ("snew_done", "so_done", "pnew_done", "sp_done"))
        so_out = [sem(f"so_out{k}") for k in range(2)]
        sp_out = sem("sp_out")
        sig_done, sg_done, normed, gated_g, gated_a, gated_b, merged, mh_done, ml_done = (
            sem(n) for n in ("sig_done", "sg_done", "normed", "gated_g", "gated_a", "gated_b", "merged", "mh_done",
                             "ml_done"))
        vs_step, sc_step, kt_step = sem("vs_step"), sem("sc_step"), sem("kt_step")
        y_turned, y_out = sem("y_turned"), sem("y_out")
        y_evac = [sem(f"y_evac{half}") for half in range(2)]

        block = ctx.enter_context(nc.Block())

        ROWS = [(c, P) for c in range(g.CH)] + [(g.CH, TS)]
        WINDOWS = [(c, slice(c * P, (c + 1) * P)) for c in range(g.CH)] + [(g.CH, slice(T - P, T))]

        @block.sync
        def _(eng):
            for c, n in ROWS:
                src = a["x_prompt"][0, c * P:(c + 1) * P, :] if c < g.CH else a["x_sample"].rearrange("b s d -> (b s) d")
                eng.dma_start(tok[0:n, c, :], src).then_inc(x_in, 16)

            def load(l, s, p, w, row0, depth, col):
                eng.wait_ge(lo_done, 2 * (l * g.SLOTS + s) + 2)
                rows = w.rearrange("(k p) c -> p k c", p=P)
                dst = raw[p][:, 0:2 * depth * P].rearrange("p (k c) -> p k c", c=2 * P)
                for k0, k1 in ((0, depth // 2), (depth // 2, depth)):
                    eng.dma_start(dst[:, k0:k1, :], rows[:, row0 + k0:row0 + k1, bass.ds(col, 2 * P)])\
                       .then_inc(raw_landed[p], 16)

            def ffn(l, s0, w_in, w_out):
                with eng.Fori(0, KF // 2) as i:
                    for p in range(2):
                        load(l, s0 + 2 * i + p, p, w_in[l], 0, KD, p * g.FF + 2 * i * P)
                with eng.Fori(0, KD // 2) as i:
                    for p in range(2):
                        load(l, s0 + KF + 2 * i + p, p, w_out[l], p * KF // 2, KF // 2, 2 * i * P)

            with eng.Fori(0, g.L) as l:
                ffn(l, g.S_F1I, a["w_ffn1_in"], a["w_ffn1_out"])
                w = a["w_in"][l]
                for n in range(NG // 2):
                    load(l, g.S_U + n, n % 2, w, 0, KD, g.C_U + 2 * n * P)
                with eng.Fori(0, 2) as i:
                    half_no = 2 * l + i
                    s0 = g.S_Q + 10 * i
                    load(l, s0, 0, w, 0, KD, g.C_Q + 2 * i * P)
                    load(l, s0 + 1, 1, w, 0, KD, g.C_K + 2 * i * P)
                    eng.wait_ge(snew_done, START + 4 * half_no)
                    eng.wait_ge(so_done, START + 4 * half_no)
                    eng.dma_start(wpq[:, :, :], a["w_pool"][l, bass.ds(2 * i, 2)].rearrange("g c n -> c g n"))\
                       .then_inc(half_in, 16)
                    eng.dma_start(qc[:, :], a["c_half"][i]).then_inc(half_in, 16)
                    for n, c in enumerate((g.C_V, g.C_G, g.C_GA, g.C_GB)):
                        for m in range(2):
                            load(l, s0 + 2 + 2 * n + m, m, w, 0, KD, c + (4 * i + 2 * m) * P)
                            for b in range(4 * n + 2 * m, 4 * n + 2 * m + 2):
                                if b < NB:
                                    eng.dma_start(st[(b % 2) * g.DK:(b % 2 + 1) * g.DK, b // 2, :, :],
                                                  a["state_ret"][l, b, bass.ds(QH * i, QH)].rearrange("h k v -> k h v"))\
                                       .then_inc(states_in, 16)
                with eng.Fori(0, KD // 4) as i:
                    for p in range(2):
                        load(l, g.S_WO + 2 * i + p, p, a["w_out"][l], 0, KD, (4 * i + 2 * p) * P)
                ffn(l, g.S_F2I, a["w_ffn2_in"], a["w_ffn2_out"])
            w = g.D // 2
            for c, n in ROWS:
                for half in range(2):
                    cols = slice(half * w, (half + 1) * w)
                    dst = o["y_prompt"][0, c * P:(c + 1) * P, cols] if c < g.CH else o["y_sample"].rearrange("b s d -> (b s) d")[:, cols]
                    eng.wait_ge(y_evac[half], c + 1)
                    eng.dma_start(dst, tok[P - n:P, c, cols]).then_inc(y_out, 16)
            eng.wait_ge(y_out, 2 * 16 * len(ROWS))
            eng.wait_ge(old_rows, 16 * g.L)
            eng.wait_ge(prow_out, START + 32 * g.L)
            for k in range(2):
                eng.wait_ge(so_out[k], START + 2 * 2 * 32 * g.L)
            eng.wait_ge(sp_out, START + 32 * g.L)

        PAIRS = g.SLOTS // 2
        HALF = g.SLOT // 2
        U_F1I, U_F1O, U_U, U_Q, U_WO, U_F2I, U_F2O = (
            n // 2 for n in (g.S_F1I, g.S_F1O, g.S_U, g.S_Q, g.S_WO, g.S_F2I, g.S_F2O))
        X_L = 3 * KD

        def number(l, u, p):
            return l * g.SLOTS + 2 * u + p

        def done(l, u, p, half=1):
            return 2 * number(l, u, p) + half + 1 + 4

        @block.tensor
        def _(eng):
            def slot(l, u, p, depth, banks, xhi, xlo, ready, k0=0, last=True):
                h = depth
                for half in range(2):
                    eng.wait_ge(lo_done, 2 * number(l, u, p) + half + 1 + 4)
                    for n in range(half * h, half * h + h):
                        k, t = divmod(n, 2)
                        if t == 0:
                            ready(k0 + k)
                        at = half * HALF + (n - half * h) * P
                        w = slice(at, at + P)
                        acc = banks[t][:, 0:T]
                        eng.matmul(acc, whi[p][:, w], xhi[:, k0 + k, :], start=(k0 + k == 0), stop=False)
                        eng.matmul(acc, whi[p][:, w], xlo[:, k0 + k, :], start=False, stop=False)
                        mm = eng.matmul(acc, wlo[p][:, w], xhi[:, k0 + k, :], start=False,
                                        stop=(last and k == depth - 1))
                    mm.then_inc(half_used, 1)

            def x_ready(l, made):
                return lambda k: eng.wait_ge(xl_done, l * X_L + made + k + 1)

            def always(k):
                pass

            def mean(n):
                eng.wait_ge(ssq_done, 9 * n)
                eng.matmul(msc[5][:, 0:T], C("mean_d"), ssq[:, :], start=True, stop=True).then_inc(mean_done, 1)

            def ffn(l, f, u_in, u_out, made, n, free0):
                def pair(i, first):
                    for p in range(2):
                        if first:
                            eng.wait_ge(x_done, START + free0[p])
                        else:
                            eng.wait_ge((gate_done, h_done)[p], f * KF + 2 * i)
                        slot(l, u_in + i, p, KD, big[2 * p:2 * p + 2], xh, xl,
                             x_ready(l, made) if first and p == 0 else always)
                        if first and p == 0:
                            mean(n)

                pair(0, True)
                with eng.Fori(1, KF // 2) as i:
                    pair(i, False)

                def h_ready(k):
                    if k in (0, KF - 2):
                        eng.wait_ge(hl_done, f * KF + (KF - 2 if k == 0 else KF))

                def pair_out(i, b):
                    for p in range(2):
                        slot(l, u_out + i, p, KF // 2, big[2 * b:2 * b + 2], hh, hl, h_ready, p * KF // 2, p == 1)

                for b in range(2):
                    eng.wait_ge((gate_done, h_done)[b], f * KF + KF)
                    pair_out(b, b)
                with eng.Fori(1, KD // 4) as e:
                    for b in range(2):
                        eng.wait_ge(x_done, START + l * X_L + made + 4 * e + 2 * b - 2)
                        pair_out(2 * e + b, b)

            eng.sem_inc(half_used, 4)
            eng.sem_inc(snew_done, START)
            eng.wait_ge(ident_in, 16)
            eng.wait_ge(vec_in, 16)
            nv = NVEC * KD
            eng.transpose(msc[7][:, 0:nv], vrow[0:nv, :], kc[0:nv, 0:nv]).then_inc(vec_turned, 1)
            eng.wait_ge(x_in, 16 * len(ROWS))
            for m in range(KD):
                if m >= 4:
                    eng.wait_ge(x_start, m - 3)
                for c, n in ROWS:
                    t = eng.transpose(big[m % 4][:, c * P:c * P + n], tok[0:n, c, m * P:(m + 1) * P], kc[0:n, 0:n])
                t.then_inc(x_turned, 1)
            eng.wait_ge(x_start, KD)
            eng.wait_ge(const_in, 16)

            with eng.Fori(0, g.L) as l:
                ffn(l, 2 * l, U_F1I, U_F1O, 0, 3 * l + 1, (l * X_L, l * X_L))

                for p in range(2):
                    eng.wait_ge(x_done, START + l * X_L + KD - 2 + 2 * p)
                    slot(l, U_U, p, KD, big[2 * p:2 * p + 2], xh, xl, x_ready(l, KD) if p == 0 else always)
                    if p == 0:
                        mean(3 * l + 2)
                        eng.wait_ge(hist_in, 16 * (l + 1))
                        for n in range(NG):
                            t = eng.transpose(msc[6][:, n * NB * BUF:(n + 1) * NB * BUF],
                                              hist[:, n * P:(n + 1) * P], kc[0:NB * BUF, 0:NB * BUF])
                        t.then_inc(hist_turned, 1)

                with eng.Fori(0, 2) as i:
                    half_no = 2 * l + i
                    Q4 = 4 * half_no

                    def pool(t, bank):
                        eng.matmul(bank[:, 0:T], wpq[:, t // 2, (t % 2) * P:(t % 2 + 1) * P], dp[:, 2 * i + t // 2, :],
                                   start=True, stop=True).then_inc(pool_done, 1)

                    def scores(h, bank):
                        r = slice(g.DK * (h % 2), g.DK * (h % 2 + 1))
                        q, k = rot[r, h // 2, :], rot[r, 2 + h // 2, :]
                        eng.matmul(bank[:, 0:SEQ], k[:, 0:P], q[:, 0:SEQ], start=True, stop=True)
                        eng.matmul(bank[:, SEQ:SEQ + P], k[:, P:SEQ], q[:, P:SEQ], start=True, stop=True)
                        eng.matmul(bank[0:TS, SEQ + P:SEQ + P + TS], k[:, SEQ:T], q[:, SEQ:T], start=True, stop=True)
                        eng.matmul(bank[:, SEQ + P + TS:SEQ + P + 2 * TS], C(f"dup{h % 2}"), rot[:, h // 2, SEQ:T],
                                   start=True, stop=True).then_inc(scores_done, 1)

                    def turn(src, bank, s):
                        for c, n in ROWS:
                            t = eng.transpose(bank[0:n, c * P:(c + 1) * P], src[:, c * P:c * P + n], C("ident"))
                        t.then_inc(s, 1)

                    def output(h, bank):
                        eng.matmul(bank[:, 0:SEQ], vt[:, 0, h, :], sc[h][:, 0:SEQ], start=True, stop=False)
                        eng.matmul(bank[:, P:SEQ], vt[:, 1, h, :], sc[h][:, SEQ:SEQ + P], start=False, stop=True)
                        eng.matmul(bank[:, SEQ:T], vs[:, h, :], scs[h][:, :], start=True, stop=False)
                        for b in range(NB // 2):
                            w = 2 * NS
                            mm = eng.matmul(bank[:, SEQ + b * w:SEQ + (b + 1) * w], st[:, b, h, :],
                                            q2[h][:, b * w:(b + 1) * w], start=False, stop=(b == NB // 2 - 1))
                        mm.then_inc(o_done, 1)

                    def omean(h, bank):
                        eng.matmul(bank[:, 0:T], C("mean_v"), osq[h % 2][:, :], start=True, stop=True)\
                           .then_inc(omean_done, 1)

                    def state(h, bank):
                        k = ksm[h % 2][:, :, :].rearrange("t b k -> t (b k)")
                        for b in range(NB // 2):
                            mm = eng.matmul(bank[:, b * P:(b + 1) * P], k[:, b * P:(b + 1) * P], vs[:, h, :],
                                            start=True, stop=True)
                        mm.then_inc(snew_done, 1)

                    def state_prompt(bank):
                        for h in range(QH):
                            for c in range(g.CH):
                                mm = eng.matmul(bank[0:g.DK, h * P:(h + 1) * P], kt[:, c, h, :], vt[:, c, h, :],
                                                start=(c == 0), stop=(c == g.CH - 1))
                        mm.then_inc(pnew_done, 1)

                    def misc(n):
                        if n == 1:
                            eng.wait_ge(half_in, HALF_IN * (2 * l + i + 1))
                            eng.wait_ge(so_done, START + Q4)
                            for t in range(2):
                                eng.wait_ge(d_done, NG * l + 2 * i + t // 2 + 1)
                                pool(t, msc[6 + t])
                        if n == 2:
                            for t in range(2, 4):
                                eng.wait_ge(d_done, NG * l + 2 * i + t // 2 + 1)
                                eng.wait_ge(pq_done, Q4 + t - 1)
                                pool(t, msc[4 + t])
                        if n == 3:
                            eng.wait_ge(rot_done, Q4 + 4)
                            eng.wait_ge(sp_done, START + half_no)
                            for h in range(2):
                                scores(h, msc[4 + h])
                            for h in range(2):
                                eng.wait_ge(z_done, START + 5 * Q4 + 2 + 5 + h)
                                eng.wait_ge(pq_done, Q4 + 3 + h)
                                turn(z[:, h, :], msc[6 + h], v_turned)
                        if n == 4:
                            for h in range(2, 4):
                                eng.wait_ge(scores_evac, Q4 + h - 1)
                                scores(h, msc[2 + h])
                            for h in range(2, 4):
                                eng.wait_ge(z_done, START + 5 * Q4 + 2 + 5 + h)
                                eng.wait_ge(vt_done, Q4 + h - 1)
                                turn(z[:, h, :], msc[4 + h], v_turned)
                        if n == 5:
                            eng.wait_ge(states_in, 16 * NB * (half_no + 1))
                            for h in range(2):
                                eng.wait_ge(scores_evac, Q4 + 3 + h)
                                eng.wait_ge(vt_done, Q4 + 1 + h)
                                output(h, msc[4 + h])
                            for t in range(2):
                                eng.wait_ge(vt_done, Q4 + 3 + t)
                                turn(rot[:, 2 + t, :], msc[6 + t], k_turned)
                        if n == 6:
                            for h in range(2):
                                eng.wait_ge(osq_done, Q4 + 1 + h)
                                omean(h, msc[4 + h])
                            for h in range(2, 4):
                                eng.wait_ge(kt_done, 2 * half_no + h - 1)
                                eng.wait_ge(ks_done, 2 * half_no + h - 1)
                                output(h, msc[4 + h])
                        if n == 7:
                            for h in range(2, 4):
                                eng.wait_ge(orms_done, Q4 + h - 1)
                                eng.wait_ge(osq_done, Q4 + 1 + h)
                                omean(h, msc[2 + h])
                            for h in range(2):
                                eng.wait_ge(ksm_done, Q4 + 1 + h)
                                state(h, msc[6 + h])
                        if n == 8:
                            for h in range(2, 4):
                                eng.wait_ge(ksm_done, Q4 + 1 + h)
                                eng.wait_ge(so_done, START + Q4 + h - 1)
                                state(h, msc[4 + h])
                            eng.wait_ge(orms_done, Q4 + 3)
                            state_prompt(msc[4])

                    for n in range(10):
                        p = n % 2
                        if n < 2:
                            eng.wait_ge(zu_done, NG * l + 2 * (n + 1))
                        eng.wait_ge(z_done, START + 5 * Q4 + 2 * n)
                        slot(l, U_Q + 5 * i + n // 2, p, KD, big[2 * p:2 * p + 2], xh, xl, always)
                        misc(n)

                for s in range(KD // 2):
                    if s < 2:
                        eng.wait_ge(z_done, START + 40 * (l + 1) + 2 * s)
                    else:
                        eng.wait_ge(x_done, START + l * X_L + KD + 2 * (s - 1))
                    slot(l, U_WO + s // 2, s % 2, KD, big[2 * (s % 2):2 * (s % 2) + 2], mh, ml,
                         (lambda k: eng.wait_ge(ml_done, START + KD * l + k + 1)) if s == 0 else always)
                    if s == 0:
                        eng.wait_ge(sp_done, START + 2 * (l + 1))
                        for n in range(NG):
                            t = eng.transpose(msc[4][:, n * P:(n + 1) * P], zu[:, n, T - P:T], C("ident"))
                        t.then_inc(prow_turned, 1)

                ffn(l, 2 * l + 1, U_F2I, U_F2O, 2 * KD, 3 * l + 3,
                    (l * X_L + 2 * KD - 2, l * X_L + 2 * KD))

            eng.wait_ge(identr_done, 1)
            eng.wait_ge(x_done, START + g.L * X_L)
            for m in range(KD):
                if m == KD - 1:
                    eng.wait_ge(ssq_done, 9 * (3 * g.L + 1))
                    for c, w in WINDOWS:
                        t = eng.matmul(msc[5][:, c:c + 1], ssq[:, w], C("mean_d")[:, 0:1], start=True, stop=True)
                    t.then_inc(mean_done, 1)
                eng.wait_ge(xl_done, g.L * X_L + m + 1)
                for c, w in WINDOWS:
                    at = ybank[2 * c + m // 4][:, (m % 4) * P:(m % 4 + 1) * P]
                    eng.matmul(at, xh[:, m, w], identr[:, :], start=True, stop=False)
                    t = eng.matmul(at, xl[:, m, w], identr[:, :], start=False, stop=True)
                t.then_inc(y_turned, 1)

        def split_size(depth):
            return depth * P

        def both_ends(eng, n, body):
            body(0, True, False)
            with eng.Fori(1, n - 1) as i:
                body(i, False, False)
            body(n - 1, False, True)

        def mixer_stored(eng, l):
            eng.wait_ge(prow_out, START + 32 * (l + 1))
            eng.wait_ge(sp_out, START + 32 * (l + 1))
            for k in range(2):
                eng.wait_ge(so_out[k], START + 2 * 2 * 32 * (l + 1))

        def next_layer(eng, l, do):
            with eng.If(l < g.L - 1):
                do(l + 1, 0)

        @block.scalar
        def _(eng):
            def hi(l, u, p, half, depth):
                n = split_size(depth)
                if half == 0:
                    eng.wait_ge(raw_landed[p], 32 * (l * PAIRS + u + 1))
                eng.wait_ge(half_used, 2 * number(l, u, p) + half + 1)
                s = slice(half * HALF, half * HALF + n)
                eng.activation(whi[p][:, s], raw[p][:, half * n:(half + 1) * n], ACT.Copy).then_inc(hi_done, 1)

            def ahead(l, u, p, depth):
                for half in range(2):
                    hi(l, u + 1, p, half, depth)

            def first_pair(l, u):
                for p in range(2):
                    for half in range(2):
                        hi(l, u, p, half, KD)

            def root(n):
                eng.wait_ge(mean_done, n)
                eng.wait_ge(r_done, START + n - 1)
                eng.activation(rb[:, :], msc[5][:, 0:T], ACT.Sqrt, bias=C("eps")).then_inc(rms_done, 1)

            def gained(l, made, m, gain):
                eng.wait_ge(x_done, START + l * X_L + made + m + 1)
                eng.activation(xh[:, m, :], x[:, m, :], ACT.Copy, scale=gl[:, bass.ds(gain * KD + m, 1)])\
                   .then_inc(xh_done, 1)

            def ffn(l, f, u_in, u_out, made, n, gain, after):
                def pair(i, first, last):
                    depth = KF // 2 if last else KD
                    ahead(l, u_in + i, 0, depth)
                    if first:
                        root(n)
                    for t in range(2):
                        eng.wait_ge(gate_done, f * KF + 2 * i + t + 1)
                        eng.activation(fs[t][:, :], fa[t][:, :], ACT.Silu).then_inc(silu_done, 1)
                    ahead(l, u_in + i, 1, depth)
                    for t in range(2):
                        eng.wait_ge(h_done, f * KF + 2 * i + t + 1)
                        eng.activation(hh[:, 2 * i + t, :], fh[t][:, :], ACT.Copy).then_inc(hh_done, 1)

                both_ends(eng, KF // 2, pair)

                def pair_out(i, first, last):
                    if last:
                        after(first_pair)
                    else:
                        for p in range(2):
                            ahead(l, u_out + i, p, KF // 2)
                    for t in range(2):
                        gained(l, made, 2 * i + t, gain)

                both_ends(eng, KD // 2, pair_out)

            for s in (sp_done, sp_out, *so_out, prow_out):
                eng.sem_inc(s, START)
            ni = g.K["ident"].stop
            eng.dma_start(kc[:, 0:ni], a["c_all"][:, 0:ni]).then_inc(ident_in, 16)
            eng.dma_start(vrow[0:NVEC * KD, :], a["c_gains"]).then_inc(vec_in, 16)
            eng.wait_ge(ident_in, 16)
            eng.activation(identr[:, :], C("ident"), ACT.Copy).then_inc(identr_done, 1)
            eng.wait_ge(vec_done, 1)
            for m in range(KD):
                eng.wait_ge(x_start, m + 1)
                eng.activation(xh[:, m, :], x[:, m, :], ACT.Copy, scale=vecT[:, m:m + 1]).then_inc(xh_done, 1)
                if m >= 4:
                    hi(0, 0, (m - 4) // 2, m % 2, KD)
            eng.dma_start(kc[:, ni:g.NK], a["c_all"][:, ni:g.NK]).then_inc(const_in, 16)
            for l in range(g.L):
                eng.dma_start(o["state_pool_sample"][l, :, 0:BUF - NS, :], a["state_pool"][l, :, NS:BUF, :])\
                   .then_inc(old_rows, 16)
            eng.wait_ge(const_in, 16)

            with eng.Fori(0, g.L) as l:
                eng.wait_ge(gl_done, l + 1)
                ffn(l, 2 * l, U_F1I, U_F1O, 0, 3 * l + 1, 1, lambda do: do(l, U_U))

                eng.wait_ge(ml_done, START + KD * l)
                eng.dma_start(hist, a["state_pool"][l].rearrange("b r c -> (b r) c")).then_inc(hist_in, 16)
                for p in range(2):
                    ahead(l, U_U, p, KD)
                    if p == 0:
                        root(3 * l + 2)
                        eng.wait_ge(hist_turned, l + 1)
                        for n in range(NG):
                            eng.activation(samples(ext[:, n, :])[:, :, 0:BUF],
                                           msc[6][:, n * NB * BUF:(n + 1) * NB * BUF].rearrange("p (b r) -> p b r", r=BUF),
                                           ACT.Copy).then_inc(hist_done, 1)
                    for n in range(2 * p, 2 * p + 2):
                        eng.wait_ge(zu_done, NG * l + n + 1)
                        eng.activation(ext[:, n, BUF:g.PSEG], zu[:, n, 0:SEQ], ACT.Copy).then_inc(ext_done, 1)
                        eng.activation(samples(ext[:, n, :])[:, :, BUF:g.SEG],
                                       zu[:, n, SEQ:T].rearrange("p (b s) -> p b s", s=NS), ACT.Copy).then_inc(ext_done, 1)

                with eng.Fori(0, 2) as i:
                    half_no = 2 * l + i
                    Q4 = 4 * half_no
                    def pool_out(t, bank):
                        eng.wait_ge(pool_done, Q4 + t + 1)
                        if t == 0:
                            eng.wait_ge(gated_b, START + Q4)
                        eng.activation(pq[:, t, :], bank[:, 0:T], ACT.Copy, scale=gl[:, bass.ds(3 * KD + 4 * i + t, 1)])\
                           .then_inc(pq_done, 1)

                    def v_out(h, bank):
                        eng.wait_ge(v_turned, Q4 + h + 1)
                        eng.activation(vt[:, :, h, :], bank[:, 0:SEQ].rearrange("p (c v) -> p c v", v=P), ACT.Copy)\
                           .then_inc(vs_step, 1)
                        eng.activation(vs[:, h, :], bank[0:TS, SEQ:SEQ + P], ACT.Copy).then_inc(vt_done, 1)

                    def sigmoid_g(h):
                        eng.wait_ge(z_done, START + 5 * Q4 + 2 + 8 + h + 1)
                        eng.wait_ge(merged, START + Q4)
                        eng.activation(sg[:, h, :], z[:, h, :], ACT.Sigmoid).then_inc(sig_done, 1)

                    def sigmoid(n):
                        eng.wait_ge(z_done, START + 5 * Q4 + 2 + n + 1)
                        eng.activation(z[:, n % 4, :], z[:, n % 4, :], ACT.Sigmoid).then_inc(sig_done, 1)

                    def o_out(h, bank):
                        eng.wait_ge(o_done, Q4 + h + 1)
                        if h == 0:
                            eng.wait_ge(ml_done, START + Q4)
                        if h == 0:
                            eng.wait_ge(d_done, NG * (l + 1))
                        eng.activation(oh[:, h, :], bank[:, 0:T], ACT.Copy).then_inc(oh_done, 1)
                        if h >= 2:
                            eng.wait_ge(omean_done, Q4 + h - 1)
                        eng.activation(osq[h % 2][:, :], bank[:, 0:T], ACT.Square).then_inc(osq_done, 1)

                    def o_root(h, bank):
                        eng.wait_ge(omean_done, Q4 + h + 1)
                        if h >= 2:
                            eng.wait_ge(normed, Q4 + h - 1)
                        eng.activation(rin[h % 2][:, :], bank[:, 0:T], ACT.Sqrt, bias=C("eps")).then_inc(orms_done, 1)

                    def state_store(h):
                        eng.wait_ge(so_done, START + Q4 + h + 1)
                        for b2 in range(2):
                            eng.dma_start(o["state_ret_sample"][l].rearrange("(b two) h k v -> two k h b v", two=2)
                                          [b2, :, 4 * i + h], so[h % 2][b2 * g.DK:(b2 + 1) * g.DK, :, :])\
                               .then_inc(so_out[h % 2], 16)

                    def swapped(t, bank):
                        if t == 0:
                            eng.wait_ge(prow_out, START + 32 * l)
                            eng.wait_ge(gated_b, START + Q4)
                        r = g.DK // 2
                        for b in range(P // r):
                            to = b ^ 1
                            ins = eng.activation(z[to * r:(to + 1) * r, t, :], bank[b * r:(b + 1) * r, 0:T], ACT.Copy)
                            ins.then_inc(swap_done, 1)

                    def upper(h):
                        eng.wait_ge(merged, START + Q4 + h + 1)
                        eng.activation(mh[:, 4 * i + h, :], oh[:, h, :], ACT.Copy).then_inc(mh_done, 1)

                    for n in range(10):
                        p, u = n % 2, U_Q + 5 * i + n // 2
                        if n == 9:
                            for h in range(2):
                                upper(h)
                        hi(l, u + 1, p, 0, KD)
                        if n < 2:
                            eng.wait_ge(half_used, done(l, u, p))
                            for t in range(2):
                                swapped(2 * n + t, big[2 * p + t])
                        if n == 9:
                            for t in (18, 19):
                                sigmoid(t)
                        hi(l, u + 1, p, 1, KD)
                        if n == 1:
                            for t in range(2):
                                pool_out(t, msc[6 + t])
                        if n == 2:
                            for t in range(2, 4):
                                pool_out(t, msc[4 + t])
                        if n == 3:
                            for h in range(2):
                                v_out(h, msc[6 + h])
                        if n == 4:
                            for h in range(2, 4):
                                v_out(h, msc[4 + h])
                            for h in range(2):
                                sigmoid_g(h)
                        if n == 5:
                            for t in range(2):
                                eng.wait_ge(kt_done, 2 * half_no + t + 1)
                                eng.activation(ks[:, 2 * t:2 * t + 2, :],
                                               msc[6 + t][0:TS, SEQ:SEQ + P].rearrange("p (h k) -> p h k", k=g.DK),
                                               ACT.Copy).then_inc(ks_done, 1)
                            for h in range(2):
                                o_out(h, msc[4 + h])
                            for h in range(2, 4):
                                sigmoid_g(h)
                        if n == 6:
                            for t in (12, 13):
                                sigmoid(t)
                            for h in range(2, 4):
                                o_out(h, msc[4 + h])
                            for h in range(2):
                                o_root(h, msc[4 + h])
                        if n == 7:
                            for h in range(2, 4):
                                o_root(h, msc[2 + h])
                            for h in range(2):
                                state_store(h)
                            for t in (14, 15):
                                sigmoid(t)
                        if n == 8:
                            for t in (16, 17):
                                sigmoid(t)
                            eng.wait_ge(pnew_done, half_no + 1)
                            eng.wait_ge(sp_out, START + 16 * half_no)
                            eng.activation(sp[:, :, :], msc[4][0:g.DK, :].rearrange("p (h v) -> p h v", v=P), ACT.Copy)\
                               .then_inc(sp_done, 1)
                            eng.wait_ge(sp_done, START + half_no + 1)
                            eng.dma_start(o["state_ret_prompt"][l, 0, bass.ds(QH * i, QH)].rearrange("h k v -> k h v"),
                                          sp[:, :, :]).then_inc(sp_out, 16)
                            for h in range(2, 4):
                                state_store(h)
                        if n == 9:
                            for h in range(2, 4):
                                upper(h)

                for s in range(KD // 2):
                    ahead(l, U_WO + s // 2, s % 2, KD)
                    for m in range(2 * s, 2 * s + 2):
                        gained(l, KD, m, 2)
                    if s == 0:
                        eng.wait_ge(prow_turned, l + 1)
                        eng.activation(prow, msc[4][:, 0:g.PIN], ACT.Copy).then_inc(prow_done, 1)
                        eng.wait_ge(prow_done, l + 1)
                        eng.dma_start(o["state_pool_prompt"][l, 0], prow[PR:PR + BUF, :]).then_inc(prow_out, 16)
                        eng.dma_start(o["state_pool_sample"][l, :, BUF - NS:BUF, :], prow[PR + BUF:P, :]).then_inc(prow_out, 16)

                mixer_stored(eng, l)
                ffn(l, 2 * l + 1, U_F2I, U_F2O, 2 * KD, 3 * l + 3, 4, lambda do: next_layer(eng, l, do))

            eng.wait_ge(mean_done, 3 * g.L + 1)
            eng.activation(rcol[:, :], msc[5][:, 0:len(ROWS)], ACT.Sqrt, bias=C("eps")).then_inc(rms_done, 1)
            eng.wait_ge(r_done, START + 3 * g.L + 1)
            eng.wait_ge(y_turned, KD)
            for c, _ in ROWS:
                eng.activation(tok[:, c, 0:g.D // 2], ybank[2 * c][:, :], ACT.Copy, scale=rcol[:, c:c + 1])\
                   .then_inc(y_evac[0], 1)

        @block.vector
        def _(eng):
            def lo(l, u, p, half, depth):
                n = split_size(depth)
                eng.wait_ge(hi_done, 2 * number(l, u, p) + half + 1)
                s = slice(half * HALF, half * HALF + n)
                eng.tensor_tensor(wlo[p][:, s], raw[p][:, half * n:(half + 1) * n], whi[p][:, s].bitcast(F32), ALU.subtract).then_inc(lo_done, 1)

            def ahead(l, u, p, half, depth):
                lo(l, u + 1, p, half, depth)

            def first_pair(l, u):
                for p in range(2):
                    for half in range(2):
                        lo(l, u, p, half, KD)

            def invert(n):
                eng.wait_ge(rms_done, n)
                eng.reciprocal(rb[:, :], rb[:, :]).then_inc(r_done, 1)

            def lower_x(l, made, m, gain):
                eng.wait_ge(xh_done, l * X_L + KD + made + m + 1)
                eng.scalar_tensor_tensor(xl[:, m, :], x[:, m, :], gl[:, bass.ds(gain * KD + m, 1)],
                                         xh[:, m, :].bitcast(F32), ALU.mult, ALU.subtract).then_inc(xl_done, 1)

            def ffn(l, f, u_in, u_out, made, n, gain, after):
                def lower_h(j, p):
                    eng.wait_ge(hh_done, f * KF + j + 1)
                    eng.tensor_tensor(hl[:, j, :], fh[p][:, :], hh[:, j, :].bitcast(F32), ALU.subtract).then_inc(hl_done, 1)

                def pair(i, first, last):
                    depth = KF // 2 if last else KD
                    ahead(l, u_in + i, 0, 0, depth)
                    if first:
                        invert(n)
                        eng.wait_ge(r_done, START + n)
                    else:
                        for t in range(2):
                            lower_h(2 * i - 2 + t, t)
                    eng.wait_ge(half_used, done(l, u_in + i, 0))
                    for t in range(2):
                        eng.tensor_tensor(fa[t][:, :], big[t][:, 0:T], rb[:, :], ALU.mult).then_inc(gate_done, 1)
                    ahead(l, u_in + i, 0, 1, depth)
                    ahead(l, u_in + i, 1, 0, depth)
                    eng.wait_ge(half_used, done(l, u_in + i, 1))
                    for t in range(2):
                        eng.wait_ge(scaled_done, f * KF + 2 * i + t + 1)
                        eng.tensor_tensor(fh[t][:, :], big[2 + t][:, 0:T], fs[t][:, :], ALU.mult).then_inc(h_done, 1)
                    ahead(l, u_in + i, 1, 1, depth)

                both_ends(eng, KF // 2, pair)
                for t in range(2):
                    lower_h(KF - 2 + t, t)

                def pair_out(i, b, last):
                    if last:
                        after(first_pair)
                    else:
                        for p in range(2):
                            for half in range(2):
                                ahead(l, u_out + i, p, half, KF // 2)
                    eng.wait_ge(half_used, done(l, u_out + i, 1))
                    for t in range(2):
                        m = 2 * i + t
                        eng.scalar_tensor_tensor(x[:, m, :], big[2 * b + t][:, 0:T], 0.5, x[:, m, :], ALU.mult, ALU.add)\
                           .then_inc(x_done, 1)
                    for t in range(2):
                        lower_x(l, made, 2 * i + t, gain)

                with eng.Fori(0, KD // 4 - 1) as e:
                    for b in range(2):
                        pair_out(2 * e + b, b, False)
                pair_out(KD // 2 - 2, 0, False)
                pair_out(KD // 2 - 1, 1, True)

            eng.sem_inc(lo_done, 4)
            eng.sem_inc(z_done, START + 2)
            for s in (x_done, r_done, so_done, ml_done, gated_b, merged):
                eng.sem_inc(s, START)
            eng.wait_ge(vec_turned, 1)
            eng.tensor_copy(vecT[:, :], msc[7][:, 0:NVEC * KD]).then_inc(vec_done, 1)
            eng.wait_ge(vec_done, 1)
            for m in range(KD + 1):
                if m < KD:
                    eng.wait_ge(x_turned, m + 1)
                    eng.tensor_copy(x[:, m, :], big[m % 4][:, 0:T]).then_inc(x_start, 1)
                if m >= 1:
                    eng.wait_ge(xh_done, m)
                    eng.scalar_tensor_tensor(xl[:, m - 1, :], x[:, m - 1, :], vecT[:, m - 1:m], xh[:, m - 1, :].bitcast(F32),
                                             ALU.mult, ALU.subtract).then_inc(xl_done, 1)
                if m >= 5:
                    lo(0, 0, (m - 5) // 2, (m - 5) % 2, KD)
            eng.wait_ge(const_in, 16)

            with eng.Fori(0, g.L) as l:
                eng.wait_ge(xl_done, l * X_L + KD)
                eng.tensor_copy(gl[:, :], vecT[:, bass.ds(l * 4 * KD, 5 * KD)]).then_inc(gl_done, 1)
                eng.wait_ge(gl_done, l + 1)
                ffn(l, 2 * l, U_F1I, U_F1O, 0, 3 * l + 1, 1, lambda do: do(l, U_U))

                for p in range(2):
                    ahead(l, U_U, p, 0, KD)
                    if p == 0:
                        invert(3 * l + 2)
                        eng.wait_ge(r_done, START + 3 * l + 2)
                    eng.wait_ge(half_used, done(l, U_U, p))
                    for t in range(2):
                        eng.tensor_tensor(zu[:, 2 * p + t, :], big[2 * p + t][:, 0:T], rb[:, :], ALU.mult)\
                           .then_inc(zu_done, 1)
                    ahead(l, U_U, p, 1, KD)

                with eng.Fori(0, 2) as i:
                    half_no = 2 * l + i
                    Q4 = 4 * half_no

                    def mask(name, h, n):
                        s = g.Q[name].start + h * n
                        return qc[:, s:s + n]

                    def rotate(t, bank):
                        eng.wait_ge(swap_done, 4 * (Q4 + t + 1))
                        kind = "qk"[t // 2]
                        eng.tensor_tensor(rot[:, t, :], bank[:, 0:T], C("cos" + kind), ALU.mult).then_inc(z_done, 1)
                        eng.tensor_tensor(z[:, t, :], z[:, t, :], C("sin" + kind), ALU.mult).then_inc(rsin_done, 1)
                        eng.wait_ge(z_done, START + 5 * Q4 + 2 + t + 1)
                        eng.wait_ge(rsin_done, Q4 + t + 1)
                        eng.tensor_tensor(rot[:, t, :], rot[:, t, :], z[:, t, :], ALU.add).then_inc(rsum_done, 1)
                        eng.wait_ge(rsum_done, Q4 + t + 1)
                        eng.tensor_tensor(rot[:, t, :], rot[:, t, :], rb[:, :], ALU.mult).then_inc(rot_done, 1)

                    def decayed(h, bank):
                        eng.wait_ge(scores_done, Q4 + h + 1)
                        m = mask("mask", h, SEQ)
                        eng.tensor_tensor(sc[h][:, 0:SEQ], bank[:, 0:SEQ], m, ALU.mult).then_inc(sc_step, 1)
                        eng.tensor_tensor(sc[h][:, SEQ:SEQ + P], bank[:, SEQ:SEQ + P], m[:, 0:P], ALU.mult).then_inc(sc_step, 1)
                        eng.tensor_tensor(scs[h][:, :], bank[0:TS, SEQ + P:SEQ + P + TS], mask("smask", h, TS)[0:TS, :],
                                          ALU.mult).then_inc(sc_step, 1)
                        eng.tensor_tensor(q2[h][:, :], bank[:, SEQ + P + TS:SEQ + P + 2 * TS], mask("qmask", h, TS),
                                          ALU.mult).then_inc(scores_evac, 1)

                    def k_out(t, bank):
                        eng.wait_ge(k_turned, 2 * half_no + t + 1)
                        wk = Q("wk").rearrange("p (c h) -> p c h", h=QH)[:, :, 2 * t:2 * t + 2]
                        for c in range(g.CH):
                            ins = eng.tensor_tensor(
                                kt[:, c, 2 * t:2 * t + 2, :],
                                bank[:, c * P:(c + 1) * P].rearrange("p (h k) -> p h k", k=g.DK),
                                wk[:, c, :].unsqueeze(2).to_broadcast([P, 2, g.DK]), ALU.mult)
                            ins.then_inc(kt_done if c == g.CH - 1 else kt_step, 1)

                    def invert_o(h):
                        eng.wait_ge(orms_done, Q4 + h + 1)
                        eng.reciprocal(rin[h % 2][:, :], rin[h % 2][:, :]).then_inc(rin_done, 1)

                    def new_state(h, bank):
                        eng.wait_ge(snew_done, START + Q4 + h + 1)
                        eng.wait_ge(so_out[h % 2], START + 32 * (2 * half_no + h // 2))
                        eng.scalar_tensor_tensor(so[h % 2][:, :, :], st[:, :, h, :], mask("decay", h, 1),
                                                 bank[:, :].rearrange("p (b v) -> p b v", v=P), ALU.mult, ALU.add)\
                           .then_inc(so_done, 1)

                    def merge(h):
                        eng.wait_ge(sig_done, 12 * half_no + 8 + h + 1)
                        eng.wait_ge(pq_done, Q4 + h + 1)
                        eng.tensor_tensor(sg[:, h, :], pq[:, h, :], z[:, h, :], ALU.mult).then_inc(gated_b, 1)
                        eng.wait_ge(gated_b, START + Q4 + h + 1)
                        eng.wait_ge(gated_a, Q4 + h + 1)
                        eng.tensor_tensor(oh[:, h, :], oh[:, h, :], sg[:, h, :], ALU.add).then_inc(merged, 1)

                    def lower(h):
                        eng.wait_ge(mh_done, Q4 + h + 1)
                        eng.tensor_tensor(ml[:, 4 * i + h, :], oh[:, h, :], mh[:, 4 * i + h, :].bitcast(F32), ALU.subtract)\
                           .then_inc(ml_done, 1)

                    def ring_free(n):
                        if n < 8:
                            eng.wait_ge(rot_done, Q4 + n - 3)
                        elif n < 12:
                            eng.wait_ge(v_turned, Q4 + n - 7)
                        elif n < 16:
                            eng.wait_ge(sg_done, Q4 + n - 11)
                        else:
                            eng.wait_ge(gated_a, Q4 + n - 15)

                    for n in range(10):
                        p, u = n % 2, U_Q + 5 * i + n // 2
                        ahead(l, u, p, 0, KD)
                        eng.wait_ge(half_used, done(l, u, p))
                        if n < 2:
                            ahead(l, u, p, 1, KD)
                            for t in range(2):
                                rotate(2 * n + t, big[2 * p + t])
                        else:
                            for t in range(2):
                                ring_free(2 * n + t)
                                eng.tensor_tensor(z[:, (2 * n + t) % 4, :], big[2 * p + t][:, 0:T], rb[:, :], ALU.mult)\
                                   .then_inc(z_done, 1)
                            ahead(l, u, p, 1, KD)
                        if n == 3:
                            eng.wait_ge(half_in, HALF_IN * (half_no + 1))
                            for h in range(2):
                                decayed(h, msc[4 + h])
                        if n == 4:
                            for h in range(2, 4):
                                decayed(h, msc[2 + h])
                        if n == 5:
                            for t in range(2):
                                k_out(t, msc[6 + t])
                        if n == 6:
                            for h in range(2):
                                invert_o(h)
                        if n == 7:
                            for h in range(2):
                                new_state(h, msc[6 + h])
                            for h in range(2, 4):
                                invert_o(h)
                        if n == 8:
                            for h in range(2, 4):
                                new_state(h, msc[4 + h])
                            for h in range(2):
                                merge(h)
                        if n == 9:
                            for h in range(2, 4):
                                merge(h)
                            for h in range(4):
                                lower(h)

                for s in range(KD // 2):
                    u, p = U_WO + s // 2, s % 2
                    ahead(l, u, p, 0, KD)
                    eng.wait_ge(half_used, done(l, u, p))
                    for t in range(2):
                        eng.tensor_tensor(x[:, 2 * s + t, :], big[2 * p + t][:, 0:T], x[:, 2 * s + t, :], ALU.add)\
                           .then_inc(x_done, 1)
                    ahead(l, u, p, 1, KD)
                    for t in range(2):
                        lower_x(l, KD, 2 * s + t, 2)

                mixer_stored(eng, l)
                ffn(l, 2 * l + 1, U_F2I, U_F2O, 2 * KD, 3 * l + 3, 4, lambda do: next_layer(eng, l, do))

            eng.wait_ge(rms_done, 3 * g.L + 1)
            eng.reciprocal(rcol[:, :], rcol[:, :]).then_inc(r_done, 1)
            eng.wait_ge(r_done, START + 3 * g.L + 1)
            eng.wait_ge(y_turned, KD)
            for c, _ in ROWS:
                eng.tensor_scalar(tok[:, c, g.D // 2:g.D], ybank[2 * c + 1][:, :], rcol[:, c:c + 1], None, ALU.mult)\
                   .then_inc(y_evac[1], 1)

        @block.gpsimd
        def _(eng):
            def squares(n, m, s, value):
                eng.wait_ge(s, value)
                eng.wait_ge(ssq_done, 9 * n + m + 1)
                eng.tensor_tensor(sqt[:, :], x[:, m, :], x[:, m, :], ALU.mult).then_inc(sq_done, 1)
                eng.wait_ge(sq_done, KD * n + m + 1)
                eng.tensor_tensor(ssq[:, :], ssq[:, :], sqt[:, :], ALU.add).then_inc(ssq_done, 1)

            def clear(n):
                eng.wait_ge(mean_done, n)
                eng.tensor_tensor(ssq[:, :], C("cosq"), C("cosq"), ALU.subtract).then_inc(ssq_done, 1)

            eng.memset(ssq[:, :], 0.0).then_inc(ssq_done, 1)
            for m in range(KD):
                squares(0, m, x_start, m + 1)
            eng.wait_ge(const_in, 16)

            def scale(l, f):
                def pair(i):
                    for t in range(2):
                        eng.wait_ge(silu_done, f * KF + 2 * i + t + 1)
                        eng.tensor_tensor(fs[t][:, :], fs[t][:, :], rb[:, :], ALU.mult).then_inc(scaled_done, 1)
                with eng.Fori(0, KF // 2) as i:
                    pair(i)

            with eng.Fori(0, g.L) as l:
                scale(l, 2 * l)
                clear(3 * l + 1)
                with eng.Fori(0, KD) as m:
                    squares(3 * l + 1, m, x_done, START + l * X_L + m + 1)

                eng.wait_ge(hist_done, NG * (l + 1))
                zero = C("cosq")[:, 0:NG * BUF].rearrange("p (n r) -> p n r", r=BUF)
                eng.tensor_tensor(ext[:, :, 0:BUF], zero, zero, ALU.subtract).then_inc(w_step, 1)
                steps = 1
                for n in range(NG):
                    eng.wait_ge(ext_done, 2 * (NG * l + n + 1))
                    src, w = ext[:, n, :], 1
                    for k in range(n + 1):
                        eng.wait_ge(w_step, W_STEPS * l + steps)
                        dst, e = win[k % 2], 2 * w - 1
                        eng.tensor_tensor(dst[:, e:g.EXT], src[:, e:g.EXT], src[:, e - w:g.EXT - w], ALU.add)\
                           .then_inc(w_step, 1)
                        steps += 1
                        src, w = dst, 2 * w
                    eng.wait_ge(w_step, W_STEPS * l + steps)
                    inv = C("inv")[:, n * 16:(n + 1) * 16]
                    eng.tensor_tensor(dp[:, n, 0:16], src[:, BUF:BUF + 16], inv, ALU.mult).then_inc(w_step, 1)
                    eng.tensor_scalar(dp[:, n, 16:SEQ], src[:, BUF + 16:g.PSEG], 1.0 / w, None, ALU.mult).then_inc(w_step, 1)
                    eng.tensor_scalar(dp[:, n, SEQ:T].rearrange("p (b s) -> p b s", s=NS),
                                      samples(src)[:, :, BUF:g.SEG], 1.0 / w, None, ALU.mult).then_inc(w_step, 1)
                    steps += 3
                    eng.wait_ge(w_step, W_STEPS * l + steps)
                    eng.tensor_tensor(dp[:, n, :], dp[:, n, :], zu[:, n, :], ALU.subtract).then_inc(d_done, 1)
                assert steps == W_STEPS

                with eng.Fori(0, 2) as i:
                    half_no = 2 * l + i
                    Q4 = 4 * half_no

                    def gated(h):
                        eng.wait_ge(sig_done, 12 * half_no + h + 1)
                        eng.tensor_tensor(sg[:, h, :], z[:, h, :], sg[:, h, :], ALU.mult).then_inc(sg_done, 1)

                    def k_masked(h):
                        eng.wait_ge(ks_done, 2 * half_no + h // 2 + 1)
                        if h >= 2:
                            eng.wait_ge(snew_done, START + Q4 + h - 1)
                        w = Q("wks").rearrange("p (h b) -> p h b", b=NB)[0:TS, h, :]
                        eng.tensor_tensor(ksm[h % 2][:, :, :], ks[:, h, :].unsqueeze(1).to_broadcast([TS, NB, g.DK]),
                                          w.unsqueeze(2).to_broadcast([TS, NB, g.DK]), ALU.mult).then_inc(ksm_done, 1)

                    def through_gates(h):
                        eng.wait_ge(rin_done, Q4 + h + 1)
                        eng.wait_ge(oh_done, Q4 + h + 1)
                        eng.tensor_tensor(oh[:, h, :], oh[:, h, :], rin[h % 2][:, :], ALU.mult).then_inc(normed, 1)
                        eng.wait_ge(normed, Q4 + h + 1)
                        eng.tensor_tensor(oh[:, h, :], oh[:, h, :], sg[:, h, :], ALU.mult).then_inc(gated_g, 1)
                        eng.wait_ge(gated_g, Q4 + h + 1)
                        eng.wait_ge(sig_done, 12 * half_no + 4 + h + 1)
                        eng.tensor_tensor(oh[:, h, :], oh[:, h, :], z[:, h, :], ALU.mult).then_inc(gated_a, 1)

                    for h in range(4):
                        gated(h)
                    eng.wait_ge(half_in, HALF_IN * (half_no + 1))
                    for h in range(2):
                        k_masked(h)
                    for h in range(2):
                        through_gates(h)
                    for h in range(2, 4):
                        k_masked(h)
                    for h in range(2, 4):
                        through_gates(h)

                for n, made in ((3 * l + 2, KD), (3 * l + 3, 2 * KD)):
                    if made == 2 * KD:
                        scale(l, 2 * l + 1)
                    clear(n)
                    with eng.Fori(0, KD) as m:
                        squares(n, m, x_done, START + l * X_L + made + m + 1)


def _constants(g):
    import numpy as np

    f = np.float32
    PAST_LEN, ROPE_BASE, EPS = 2048, 10000.0, 1e-6
    POOL_WINDOWS = (2, 4, 8, 16)
    kc = np.zeros((P, g.NK), f)

    def put(name, table):
        kc[:, g.K[name]] = table

    put("ident", np.eye(P))
    put("mean_d", 1.0 / g.D)
    put("mean_v", 1.0 / g.DV)
    half = g.DK // 2
    row = np.arange(P)
    for par in range(2):
        put(f"dup{par}", (row[:, None] == par * g.DK + row[None, :] % g.DK).astype(f))
    pos = np.concatenate([np.arange(g.SEQ), np.tile(PAST_LEN + np.arange(g.NS), g.NB)]).astype(f)
    inv = np.power(f(ROPE_BASE), -np.linspace(0.0, 1.0, half, dtype=f)).astype(f)
    ang = (pos[None, :] * inv[row % half][:, None]).astype(f)
    sign = np.where(row % g.DK < half, -1.0, 1.0).astype(f)[:, None]
    cos, sin = np.cos(ang), np.sin(ang) * sign
    put("cosq", cos)
    put("sinq", sin)
    put("cosk", cos * f(g.DK ** -0.5))
    put("sink", sin * f(g.DK ** -0.5))
    t = np.arange(16)
    put("inv", np.concatenate([1.0 / np.minimum(t + 1, w) for w in POOL_WINDOWS])[None, :])
    put("eps", EPS)

    lg = np.log1p(-np.exp2(-5.0 - np.arange(g.H, dtype=np.float64)))
    qc = np.zeros((2, P, g.NQ), f)
    j, i = np.arange(P), np.arange(g.SEQ)
    tok = np.arange(g.TS)
    b, s = tok // g.NS, tok % g.NS
    for h in range(g.H):
        half_no, hh = divmod(h, g.QH)

        def half_put(name, n, table, rows=P):
            at = g.Q[name].start + hh * n
            qc[half_no, 0:rows, at:at + n] = table

        dist = i[None, :] - j[:, None]
        half_put("mask", g.SEQ, np.where(dist >= 0, np.exp(lg[h] * np.maximum(dist, 0)), 0.0))
        dist = s[None, :] - s[:, None]
        same = b[None, :] == b[:, None]
        half_put("smask", g.TS, np.where(same & (dist >= 0), np.exp(lg[h] * np.maximum(dist, 0)), 0.0), g.TS)
        half_put("qmask", g.TS, np.where(b[None, :] % 2 == (row // g.DK)[:, None], np.exp(lg[h] * (s + 1.0))[None, :], 0.0))
        half_put("wks", g.NB, np.where(b[:, None] == np.arange(g.NB)[None, :], np.exp(lg[h] * (g.NS - 1.0 - s))[:, None], 0.0), g.TS)
        half_put("decay", 1, np.exp(lg[h] * g.NS))
        for c in range(g.CH):
            qc[half_no, :, g.Q["wk"].start + c * g.QH + hh] = np.exp(lg[h] * (g.SEQ - 1.0 - (c * P + j)))
    return kc, qc


def kernel(**inputs):
    import numpy as np
    import concourse.bacc as bacc
    from concourse.bass_utils import run_bass_kernel_spmd

    nc = bacc.Bacc("TRN2", target_bir_lowering=False, num_devices=1)
    g = plan({n: v.shape for n, v in inputs.items()})
    kc, qc = _constants(g)
    arrays = {n: np.ascontiguousarray(inputs[n]) for n in (
        "x_prompt", "x_sample", "state_ret", "state_pool", "w_ffn1_in", "w_ffn1_out", "w_in", "w_pool", "w_out",
        "w_ffn2_in", "w_ffn2_out")}
    rows = [np.asarray(inputs[n])[l] for l in range(g.L) for n in ("norm_ffn1", "norm_mix", "norm_ffn2", "pool_scale")]
    arrays["c_gains"] = np.ascontiguousarray(np.stack(rows + [np.asarray(inputs["norm_final"])]).reshape(-1, P))
    arrays["c_all"], arrays["c_half"] = kc, qc
    outs = {
        "y_prompt": (1, g.SEQ, g.D), "y_sample": (g.NB, g.NS, g.D),
        "state_ret_prompt": (g.L, 1, g.H, g.DK, g.DV), "state_ret_sample": (g.L, g.NB, g.H, g.DK, g.DV),
        "state_pool_prompt": (g.L, 1, g.BUF, g.PIN), "state_pool_sample": (g.L, g.NB, g.BUF, g.PIN),
    }
    a = {n: nc.dram_tensor("in_" + n, v.shape, F32, kind="ExternalInput").ap() for n, v in arrays.items()}
    o = {n: nc.dram_tensor("out_" + n, s, F32, kind="ExternalOutput").ap() for n, s in outs.items()}
    decoder_step(nc, g, a, o)
    r = run_bass_kernel_spmd(nc, [{"in_" + n: v for n, v in arrays.items()}], core_ids=[0])
    return tuple(r.results[0]["out_" + n] for n in outs)
```

```python
from contextlib import ExitStack

import concourse.bass as bass
from concourse import mybir

F32 = mybir.dt.float32
F32R = mybir.dt.float32r
ALU = mybir.AluOpType
ACT = mybir.ActivationFunctionType

P = 128


def plan(shapes):
    class G:
        pass

    g = G()
    _, g.SEQ, g.D = shapes["x_prompt"]
    g.NB, g.NS, _ = shapes["x_sample"]
    g.L, _, g.H, g.DK, g.DV = shapes["state_ret"]
    g.BUF, g.PIN = shapes["state_pool"][2:]
    g.FF = shapes["w_ffn1_out"][1]
    g.NG = shapes["w_pool"][1]
    g.KD = g.D // P
    g.KF = g.FF // P
    g.TS = g.NB * g.NS
    g.T = g.SEQ + g.TS
    g.CH = g.SEQ // P
    g.QH = g.H // 2
    g.UK = 2 * g.KD * P
    g.UF = g.KF * P
    g.SLOT = max(g.UK, g.UF)
    g.SEG = g.BUF + g.NS
    g.PSEG = g.BUF + g.SEQ
    g.EXT = g.PSEG + g.NB * g.SEG
    g.S_F1I = 0
    g.S_F1O = g.S_F1I + g.KF
    g.S_U = g.S_F1O + g.KD
    g.S_Q = g.S_U + g.NG // 2
    g.S_WO = g.S_Q + 20
    g.S_F2I = g.S_WO + g.KD // 2
    g.S_F2O = g.S_F2I + g.KF
    g.SLOTS = g.S_F2O + g.KD
    qk, v = g.H * g.DK, g.H * g.DV
    g.C_Q, g.C_K, g.C_V, g.C_G = 0, qk, 2 * qk, 2 * qk + v
    g.C_U = 2 * qk + 2 * v
    g.C_GA = g.C_U + g.PIN
    g.C_GB = g.C_GA + g.D
    at = 0
    g.K = {}
    for name, n in (("ident", P), ("mean_d", P), ("dup0", P), ("dup1", P), ("cos", g.T), ("sin", g.T),
                    ("inv", g.NG * 16), ("eps", 1)):
        g.K[name] = slice(at, at + n)
        at += n
    g.NK = at
    at = 0
    g.Q = {}
    for name, n in (("mask", g.QH * g.SEQ), ("smask", g.QH * g.TS), ("qmask", g.QH * g.TS),
                    ("wk", g.CH * g.QH), ("wks", g.QH), ("seq", g.NB), ("decay", g.QH)):
        g.Q[name] = slice(at, at + n)
        at += n
    g.NQ = at
    assert g.SEQ == 2 * P and g.DV == P and 2 * g.DK == P and g.QH == 4 and g.NG == 4
    assert g.TS == 32 and g.KF % 2 == 0 and g.SLOTS % 2 == 0 and g.PIN == g.NG * P and g.D == g.H * g.DV
    return g


def decoder_step(nc, g, a, o):
    T, TS, SEQ, KD, KF, NB, NS, NG, QH, BUF = g.T, g.TS, g.SEQ, g.KD, g.KF, g.NB, g.NS, g.NG, g.QH, g.BUF
    ctx = ExitStack()
    with ctx:
        def sem(name):
            return ctx.enter_context(nc.semaphore(name))

        def sb(name, shape, dt=F32, stack=ctx):
            return stack.enter_context(nc.sbuf_tensor(name, shape, dt))

        raw = [sb(f"raw{p}", [P, g.SLOT]) for p in range(2)]
        whi = [sb(f"whi{p}", [P, g.SLOT], F32R) for p in range(2)]
        wlo = [sb(f"wlo{p}", [P, g.SLOT], F32R) for p in range(2)]
        x = sb("x", [P, KD, T])
        xh = sb("xh", [P, KD, T], F32R)
        xl = sb("xl", [P, KD, T], F32R)
        rb = sb("rb", [P, T])
        ssq = sb("ssq", [P, T])
        sqt = sb("sqt", [P, T])
        kc = sb("kc", [P, g.NK])
        identr = sb("identr", [P, P], F32R)
        meanr = sb("meanr", [P, P], F32R)
        rcol = sb("rcol", [P, g.CH + 1])
        NVEC = 4 * g.L + 1
        vecT = sb("vecT", [P, NVEC * KD])
        gl = sb("gl", [P, 5 * KD])
        over = ExitStack()
        hh = sb("hh", [P, KF, T], F32R, over)
        hl = sb("hl", [P, KF, T], F32R, over)
        fa = [sb(f"fa{p}", [P, T], F32, over) for p in range(2)]
        fs = [sb(f"fs{p}", [P, T], F32, over) for p in range(2)]
        fh = [sb(f"fh{p}", [P, T], F32, over) for p in range(2)]
        over.close()
        over = ExitStack()
        tok = sb("tok", [P, g.CH + 1, g.D], F32, over)
        vrow = sb("vrow", [P, P], F32, over)
        over.close()
        mh = sb("mh", [P, KD, T], F32R)
        ml = sb("ml", [P, KD, T], F32R)
        zu = sb("zu", [P, NG, T])
        ext = sb("ext", [P, NG, g.EXT])
        dp = sb("dp", [P, NG, T])
        pq = sb("pq", [P, 4, T])
        z = sb("z", [P, 4, T])
        rot = sb("rot", [P, 4, T])
        vt = sb("vt", [P, g.CH, QH, P])
        vs = sb("vs", [3 * TS, QH, P], F32R)
        kt = sb("kt", [P, g.CH, QH, g.DK])
        ks = sb("ks", [3 * TS, QH, g.DK], F32R)
        ksm = [sb(f"ksm{k}", [3 * TS, NB, g.DK], F32R) for k in range(2)]
        sc = [sb(f"sc{h}", [P, SEQ + P]) for h in range(QH)]
        scs = [sb(f"scs{h}", [2 * TS, TS]) for h in range(QH)]
        q2 = [sb(f"q2{h}", [P, TS]) for h in range(QH)]
        oh = sb("oh", [P, QH, T])
        over = ExitStack()
        win = [sb(f"win{k}", [P, g.EXT], F32, over) for k in range(2)]
        over.close()
        over = ExitStack()
        osq = [sb(f"osq{k}", [P, T], F32, over) for k in range(2)]
        over.close()
        osl = [sb(f"osl{k}", [P, T], F32R) for k in range(2)]
        rin = [sb(f"rin{k}", [P, T]) for k in range(2)]
        osh = [sb(f"osh{k}", [P, T], F32R) for k in range(2)]
        sg = sb("sg", [P, QH, T])
        st = sb("st", [P, NB // 2, QH, P])
        so = [sb(f"so{k}", [P, NB // 2, P]) for k in range(2)]
        sp = sb("sp", [g.DK, QH, P])
        wpq = sb("wpq", [P, 2, 2 * P])
        qc = sb("qc", [P, g.NQ])
        hist = oh[:, :, :].rearrange("p h t -> p (h t)")[0:NB * BUF, 0:g.PIN]
        PR = P - TS - BUF
        prow = z[:, :, :].rearrange("p n t -> p (n t)")[:, 0:g.PIN]

        HALF_IN = 32
        W_STEPS = 1 + NG * (NG + 1) // 2 + 3 * NG

        def samples(row):
            return row[:, g.PSEG:g.EXT].rearrange("p (b r) -> p b r", r=g.SEG)

        big = [ctx.enter_context(nc.psum_tensor(f"acc{k}", [P, 512], F32)) for k in range(4)]
        msc = [None] * 4 + [ctx.enter_context(nc.psum_tensor(f"misc{k}", [P, 512], F32)) for k in range(4, 8)]

        ybank = [big[0], msc[7], big[1], big[2], msc[6], big[3]]

        def C(name):
            return kc[:, g.K[name]]

        def Q(name):
            return qc[:, g.Q[name]]

        START = 3

        raw_landed = [sem(f"raw_landed{p}") for p in range(2)]
        hi_done = sem("hi_done")
        lo_done = sem("lo_done")
        half_used = sem("half_used")
        ident_in, const_in, x_in, vec_in, old_rows = (
            sem(n) for n in ("ident_in", "const_in", "x_in", "vec_in", "old_rows"))
        exact_done = sem("exact_done")
        x_turned, x_start, vec_turned, vec_done, gl_done = (
            sem(n) for n in ("x_turned", "x_start", "vec_turned", "vec_done", "gl_done"))
        x_done, xh_done, xl_done = sem("x_done"), sem("xh_done"), sem("xl_done")
        sq_done, ssq_done = sem("sq_done"), sem("ssq_done")
        mean_done, rms_done, r_done = sem("mean_done"), sem("rms_done"), sem("r_done")
        gate_done, scaled_done, silu_done, h_done, hh_done, hl_done = (
            sem(n) for n in ("gate_done", "scaled_done", "silu_done", "h_done", "hh_done", "hl_done"))
        hist_in, hist_turned, hist_done, zu_done, ext_done, w_step, d_tmp, d_done = (
            sem(n) for n in ("hist_in", "hist_turned", "hist_done", "zu_done", "ext_done", "w_step", "d_tmp", "d_done"))
        pool_done, pq_done, prow_turned, prow_done, prow_out = (
            sem(n) for n in ("pool_done", "pq_done", "prow_turned", "prow_done", "prow_out"))
        half_in, states_in, z_done, swap_done, sin_done, rsum_done, rot_done = (
            sem(n) for n in ("half_in", "states_in", "z_done", "swap_done", "sin_done", "rsum_done", "rot_done"))
        scores_done, scores_evac, v_turned, vt_done, k_turned, kt_done, ks_done, ksm_done = (
            sem(n) for n in ("scores_done", "scores_evac", "v_turned", "vt_done", "k_turned", "kt_done", "ks_done",
                             "ksm_done"))
        o_done, oh_done, osq_done, osh_done, osl_done, omean_done, orms_done, rin_done = (
            sem(n) for n in ("o_done", "oh_done", "osq_done", "osh_done", "osl_done", "omean_done", "orms_done",
                             "rin_done"))
        vlo_done, klo_done, khi_step, klo_step = (sem(n) for n in ("vlo_done", "klo_done", "khi_step", "klo_step"))
        snew_done, so_done, pnew_done, sp_done = (sem(n) for n in ("snew_done", "so_done", "pnew_done", "sp_done"))
        so_free = sem("so_free")
        so_out = [sem(f"so_out{k}") for k in range(2)]
        sp_out = sem("sp_out")
        sig_done, sg_done, normed, gated_g, gated_a, gated_b, merged, mh_done, ml_done = (
            sem(n) for n in ("sig_done", "sg_done", "normed", "gated_g", "gated_a", "gated_b", "merged", "mh_done",
                             "ml_done"))
        vs_step, sc_step, kt_step = sem("vs_step"), sem("sc_step"), sem("kt_step")
        y_turned, y_out = sem("y_turned"), sem("y_out")
        y_evac = [sem(f"y_evac{half}") for half in range(2)]

        block = ctx.enter_context(nc.Block())

        ROWS = [(c, P) for c in range(g.CH)] + [(g.CH, TS)]
        WINDOWS = [(c, slice(c * P, (c + 1) * P)) for c in range(g.CH)] + [(g.CH, slice(T - P, T))]

        @block.sync
        def _(eng):
            for c, n in ROWS:
                src = a["x_prompt"][0, c * P:(c + 1) * P, :] if c < g.CH else a["x_sample"].rearrange("b s d -> (b s) d")
                eng.dma_start(tok[0:n, c, :], src).then_inc(x_in, 16)

            def load(l, s, p, w, row0, depth, col):
                eng.wait_ge(lo_done, 2 * (l * g.SLOTS + s) + 2)
                rows = w.rearrange("(k p) c -> p k c", p=P)
                dst = raw[p][:, 0:2 * depth * P].rearrange("p (k c) -> p k c", c=2 * P)
                for k0, k1 in ((0, depth // 2), (depth // 2, depth)):
                    eng.dma_start(dst[:, k0:k1, :], rows[:, row0 + k0:row0 + k1, bass.ds(col, 2 * P)])\
                       .then_inc(raw_landed[p], 16)

            def ffn(l, s0, w_in, w_out):
                with eng.Fori(0, KF // 2) as i:
                    for p in range(2):
                        load(l, s0 + 2 * i + p, p, w_in[l], 0, KD, p * g.FF + 2 * i * P)
                with eng.Fori(0, KD // 2) as i:
                    for p in range(2):
                        load(l, s0 + KF + 2 * i + p, p, w_out[l], p * KF // 2, KF // 2, 2 * i * P)

            with eng.Fori(0, g.L) as l:
                ffn(l, g.S_F1I, a["w_ffn1_in"], a["w_ffn1_out"])
                w = a["w_in"][l]
                for n in range(NG // 2):
                    load(l, g.S_U + n, n % 2, w, 0, KD, g.C_U + 2 * n * P)
                with eng.Fori(0, 2) as i:
                    half_no = 2 * l + i
                    s0 = g.S_Q + 10 * i
                    load(l, s0, 0, w, 0, KD, g.C_Q + 2 * i * P)
                    load(l, s0 + 1, 1, w, 0, KD, g.C_K + 2 * i * P)
                    for n, c in enumerate((g.C_V, g.C_G, g.C_GA, g.C_GB)):
                        for m in range(2):
                            load(l, s0 + 2 + 2 * n + m, m, w, 0, KD, c + (4 * i + 2 * m) * P)
                            for b in range(4 * n + 2 * m - 4, 4 * n + 2 * m - 2):
                                if 0 <= b < NB:
                                    eng.dma_start(st[(b % 2) * g.DK:(b % 2 + 1) * g.DK, b // 2, :, :],
                                                  a["state_ret"][l, b, bass.ds(QH * i, QH)].rearrange("h k v -> k h v"))\
                                       .then_inc(states_in, 16)
                        if n == 0:
                            eng.wait_ge(snew_done, START + 4 * half_no)
                            eng.wait_ge(so_done, START + 4 * half_no)
                            eng.dma_start(wpq[:, :, :], a["w_pool"][l, bass.ds(2 * i, 2)].rearrange("g c n -> c g n"))\
                               .then_inc(half_in, 16)
                            eng.dma_start(qc[:, :], a["c_half"][i]).then_inc(half_in, 16)
                with eng.Fori(0, KD // 4) as i:
                    for p in range(2):
                        load(l, g.S_WO + 2 * i + p, p, a["w_out"][l], 0, KD, (4 * i + 2 * p) * P)
                ffn(l, g.S_F2I, a["w_ffn2_in"], a["w_ffn2_out"])
            w = g.D // 2
            for c, n in ROWS:
                for half in range(2):
                    cols = slice(half * w, (half + 1) * w)
                    dst = o["y_prompt"][0, c * P:(c + 1) * P, cols] if c < g.CH else o["y_sample"].rearrange("b s d -> (b s) d")[:, cols]
                    eng.wait_ge(y_evac[half], c + 1)
                    eng.dma_start(dst, tok[P - n:P, c, cols]).then_inc(y_out, 16)
            eng.wait_ge(y_out, 2 * 16 * len(ROWS))
            eng.wait_ge(old_rows, 16 * g.L)
            eng.wait_ge(prow_out, START + 32 * g.L)
            for k in range(2):
                eng.wait_ge(so_out[k], 2 * 2 * 32 * g.L)
            eng.wait_ge(sp_out, START + 32 * g.L)

        PAIRS = g.SLOTS // 2
        HALF = g.SLOT // 2
        U_F1I, U_F1O, U_U, U_Q, U_WO, U_F2I, U_F2O = (
            n // 2 for n in (g.S_F1I, g.S_F1O, g.S_U, g.S_Q, g.S_WO, g.S_F2I, g.S_F2O))
        X_L = 3 * KD

        def number(l, u, p):
            return l * g.SLOTS + 2 * u + p

        def done(l, u, p, half=1):
            return 2 * number(l, u, p) + half + 1 + 4

        @block.tensor
        def _(eng):
            def slot(l, u, p, depth, banks, xhi, xlo, ready, k0=0, last=True):
                h = depth
                for half in range(2):
                    eng.wait_ge(lo_done, 2 * number(l, u, p) + half + 1 + 4)
                    for n in range(half * h, half * h + h):
                        k, t = divmod(n, 2)
                        if t == 0:
                            ready(k0 + k)
                        at = half * HALF + (n - half * h) * P
                        w = slice(at, at + P)
                        acc = banks[t][:, 0:T]
                        eng.matmul(acc, whi[p][:, w], xhi[:, k0 + k, :], start=(k0 + k == 0), stop=False)
                        eng.matmul(acc, whi[p][:, w], xlo[:, k0 + k, :], start=False, stop=False)
                        mm = eng.matmul(acc, wlo[p][:, w], xhi[:, k0 + k, :], start=False,
                                        stop=(last and k == depth - 1))
                    mm.then_inc(half_used, 1)

            def x_ready(l, made):
                return lambda k: eng.wait_ge(xl_done, l * X_L + made + k + 1)

            def always(k):
                pass

            def mean(n):
                eng.wait_ge(const_in, 16)
                eng.wait_ge(ssq_done, 9 * n)
                eng.matmul(msc[5][:, 0:T], C("mean_d"), ssq[:, :], start=True, stop=True).then_inc(mean_done, 1)

            def ffn(l, f, u_in, u_out, made, n, free0):
                def mean_within(k):
                    if k == 1:
                        mean(n)

                def pair(i, first):
                    for p in range(2):
                        if first:
                            eng.wait_ge(x_done, START + free0[p])
                        else:
                            eng.wait_ge((gate_done, h_done)[p], f * KF + 2 * i)
                        slot(l, u_in + i, p, KD, big[2 * p:2 * p + 2], xh, xl,
                             always if not first else x_ready(l, made) if p == 0 else mean_within)

                pair(0, True)
                with eng.Fori(1, KF // 2) as i:
                    pair(i, False)

                def h_ready(k):
                    if k in (0, KF - 2):
                        eng.wait_ge(hl_done, f * KF + (KF - 2 if k == 0 else KF))

                def pair_out(i, b):
                    for p in range(2):
                        slot(l, u_out + i, p, KF // 2, big[2 * b:2 * b + 2], hh, hl, h_ready, p * KF // 2, p == 1)

                for b in range(2):
                    eng.wait_ge((gate_done, h_done)[b], f * KF + KF)
                    pair_out(b, b)
                with eng.Fori(1, KD // 4) as e:
                    for b in range(2):
                        eng.wait_ge(x_done, START + l * X_L + made + 4 * e + 2 * b - 2)
                        pair_out(2 * e + b, b)

            eng.sem_inc(half_used, 4)
            eng.sem_inc(snew_done, START)
            eng.wait_ge(ident_in, 16)
            eng.wait_ge(vec_in, 16)
            nv = NVEC * KD
            eng.transpose(msc[7][:, 0:nv], vrow[0:nv, :], kc[0:nv, 0:nv]).then_inc(vec_turned, 1)
            eng.wait_ge(x_in, 16 * len(ROWS))
            for m in range(KD):
                if m >= 4:
                    eng.wait_ge(x_start, m - 3)
                for c, n in ROWS:
                    t = eng.transpose(big[m % 4][:, c * P:c * P + n], tok[0:n, c, m * P:(m + 1) * P], kc[0:n, 0:n])
                t.then_inc(x_turned, 1)
            eng.wait_ge(x_start, KD - 2)

            with eng.Fori(0, g.L) as l:
                ffn(l, 2 * l, U_F1I, U_F1O, 0, 3 * l + 1, (l * X_L - 2, l * X_L))

                def mean_and_history(k):
                    if k == 1:
                        mean(3 * l + 2)
                    if k == KD - 2:
                        eng.wait_ge(hist_in, 16 * (l + 1))
                        for n in range(NG):
                            t = eng.transpose(msc[6][:, n * NB * BUF:(n + 1) * NB * BUF],
                                              hist[:, n * P:(n + 1) * P], kc[0:NB * BUF, 0:NB * BUF])
                        t.then_inc(hist_turned, 1)

                for p in range(2):
                    eng.wait_ge(x_done, START + l * X_L + KD - 2 + 2 * p)
                    slot(l, U_U, p, KD, big[2 * p:2 * p + 2], xh, xl,
                         x_ready(l, KD) if p == 0 else mean_and_history)

                with eng.Fori(0, 2) as i:
                    half_no = 2 * l + i
                    Q4 = 4 * half_no

                    def pool(t, bank):
                        eng.matmul(bank[:, 0:T], wpq[:, t // 2, (t % 2) * P:(t % 2 + 1) * P], dp[:, 2 * i + t // 2, :],
                                   start=True, stop=True).then_inc(pool_done, 1)

                    def scores(h, bank):
                        r = slice(g.DK * (h % 2), g.DK * (h % 2 + 1))
                        q, k = rot[r, h // 2, :], rot[r, 2 + h // 2, :]
                        eng.matmul(bank[:, 0:SEQ], k[:, 0:P], q[:, 0:SEQ], start=True, stop=True)
                        eng.matmul(bank[:, SEQ:SEQ + P], k[:, P:SEQ], q[:, P:SEQ], start=True, stop=True)
                        eng.matmul(bank[0:TS, SEQ + P:SEQ + P + TS], k[:, SEQ:T], q[:, SEQ:T], start=True, stop=True)
                        eng.matmul(bank[:, SEQ + P + TS:SEQ + P + 2 * TS], C(f"dup{h % 2}"), rot[:, h // 2, SEQ:T],
                                   start=True, stop=True).then_inc(scores_done, 1)

                    def turn(src, bank, s):
                        for c, n in ROWS:
                            t = eng.transpose(bank[0:n, c * P:(c + 1) * P], src[:, c * P:c * P + n], C("ident"))
                        t.then_inc(s, 1)

                    def output(h, bank):
                        eng.matmul(bank[:, 0:SEQ], vt[:, 0, h, :], sc[h][:, 0:SEQ], start=True, stop=False)
                        eng.matmul(bank[:, P:SEQ], vt[:, 1, h, :], sc[h][:, SEQ:SEQ + P], start=False, stop=True)
                        eng.matmul(bank[:, SEQ:T], vs[0:2 * TS, h, :].bitcast(F32), scs[h][:, :], start=True, stop=False)
                        for b in range(NB // 2):
                            w = 2 * NS
                            mm = eng.matmul(bank[:, SEQ + b * w:SEQ + (b + 1) * w], st[:, b, h, :],
                                            q2[h][:, b * w:(b + 1) * w], start=False, stop=(b == NB // 2 - 1))
                        mm.then_inc(o_done, 1)

                    def omean(h, bank):
                        eng.matmul(bank[:, 0:T], meanr[:, :], osh[h % 2][:, :], start=True, stop=False)
                        eng.matmul(bank[:, 0:T], meanr[:, :], osl[h % 2][:, :], start=False, stop=True)\
                           .then_inc(omean_done, 1)

                    def state(h, bank):
                        k = ksm[h % 2][:, :, :].rearrange("t b k -> t (b k)")
                        for b in range(NB // 2):
                            mm = eng.matmul(bank[:, b * P:(b + 1) * P], k[:, b * P:(b + 1) * P], vs[:, h, :],
                                            start=True, stop=True)
                        mm.then_inc(snew_done, 1)

                    def state_prompt(bank):
                        for h in range(QH):
                            for c in range(g.CH):
                                mm = eng.matmul(bank[0:g.DK, h * P:(h + 1) * P], kt[:, c, h, :], vt[:, c, h, :],
                                                start=(c == 0), stop=(c == g.CH - 1))
                        mm.then_inc(pnew_done, 1)

                    def misc(n):
                        if n == 2:
                            eng.wait_ge(half_in, HALF_IN * (2 * l + i + 1))
                            eng.wait_ge(so_done, START + Q4)
                            eng.wait_ge(sp_done, START + half_no)
                            for t in range(4):
                                eng.wait_ge(d_done, NG * l + 2 * i + t // 2 + 1)
                                pool(t, msc[4 + (t + 2) % 4])
                        if n == 3:
                            eng.wait_ge(rot_done, Q4 + 4)
                            for h in range(2):
                                eng.wait_ge(pq_done, Q4 + 3 + h)
                                scores(h, msc[4 + h])
                            for h in range(2):
                                eng.wait_ge(z_done, START + 5 * Q4 + 2 + 5 + h)
                                turn(z[:, h, :], msc[6 + h], v_turned)
                        if n == 4:
                            for h in range(2, 4):
                                eng.wait_ge(scores_evac, Q4 + h - 1)
                                scores(h, msc[2 + h])
                            for h in range(2, 4):
                                eng.wait_ge(z_done, START + 5 * Q4 + 2 + 5 + h)
                                eng.wait_ge(vlo_done, Q4 + h - 1)
                                turn(z[:, h, :], msc[4 + h], v_turned)
                        if n == 5:
                            eng.wait_ge(states_in, 16 * NB * (half_no + 1))
                            for h in range(2):
                                eng.wait_ge(scores_evac, Q4 + 3 + h)
                                eng.wait_ge(vlo_done, Q4 + 1 + h)
                                output(h, msc[4 + h])
                            for t in range(2):
                                eng.wait_ge(vlo_done, Q4 + 3 + t)
                                turn(rot[:, 2 + t, :], msc[6 + t], k_turned)
                        if n == 6:
                            for h in range(2):
                                eng.wait_ge(osl_done, Q4 + 1 + h)
                                omean(h, msc[4 + h])
                            for h in range(2, 4):
                                eng.wait_ge(kt_done, 2 * half_no + h - 1)
                                eng.wait_ge(klo_done, 2 * half_no + h - 1)
                                output(h, msc[4 + h])
                        if n == 7:
                            for h in range(2, 4):
                                eng.wait_ge(orms_done, Q4 + h - 1)
                                eng.wait_ge(osl_done, Q4 + 1 + h)
                                omean(h, msc[2 + h])
                            for h in range(2):
                                eng.wait_ge(ksm_done, Q4 + 1 + h)
                                state(h, msc[6 + h])
                        if n == 8:
                            for h in range(2, 4):
                                eng.wait_ge(ksm_done, Q4 + 1 + h)
                                eng.wait_ge(so_done, START + Q4 + h - 1)
                                state(h, msc[4 + h])
                            eng.wait_ge(orms_done, Q4 + 3)
                            state_prompt(msc[4])

                    for n in range(10):
                        p = n % 2
                        if n < 2:
                            eng.wait_ge(zu_done, NG * l + 2 * (n + 1))
                        eng.wait_ge(z_done, START + 5 * Q4 + 2 * n)
                        slot(l, U_Q + 5 * i + n // 2, p, KD, big[2 * p:2 * p + 2], xh, xl, always)
                        misc(n)

                for s in range(KD // 2):
                    if s < 2:
                        eng.wait_ge(z_done, START + 40 * (l + 1) + 2 * s)
                    else:
                        eng.wait_ge(x_done, START + l * X_L + KD + 2 * (s - 1))
                    slot(l, U_WO + s // 2, s % 2, KD, big[2 * (s % 2):2 * (s % 2) + 2], mh, ml,
                         (lambda k: eng.wait_ge(ml_done, START + KD * l + k + 1)) if s == 0 else always)
                    if s == 0:
                        eng.wait_ge(sp_done, START + 2 * (l + 1))
                        for n in range(NG):
                            t = eng.transpose(msc[4][:, n * P:(n + 1) * P], zu[:, n, T - P:T], C("ident"))
                        t.then_inc(prow_turned, 1)

                ffn(l, 2 * l + 1, U_F2I, U_F2O, 2 * KD, 3 * l + 3,
                    (l * X_L + 2 * KD - 2, l * X_L + 2 * KD))

            eng.wait_ge(exact_done, 2)
            eng.wait_ge(x_done, START + g.L * X_L - 2)
            for m in range(KD):
                if m == KD // 2:
                    eng.wait_ge(x_done, START + g.L * X_L)
                if m == KD - 1:
                    eng.wait_ge(ssq_done, 9 * (3 * g.L + 1))
                    for c, w in WINDOWS:
                        t = eng.matmul(msc[5][:, c:c + 1], ssq[:, w], C("mean_d")[:, 0:1], start=True, stop=True)
                    t.then_inc(mean_done, 1)
                eng.wait_ge(xl_done, g.L * X_L + m + 1)
                for c, w in WINDOWS:
                    at = ybank[2 * c + m // 4][:, (m % 4) * P:(m % 4 + 1) * P]
                    eng.matmul(at, xh[:, m, w], identr[:, :], start=True, stop=False)
                    t = eng.matmul(at, xl[:, m, w], identr[:, :], start=False, stop=True)
                t.then_inc(y_turned, 1)

        def split_size(depth):
            return depth * P

        def both_ends(eng, n, body):
            body(0, True, False)
            with eng.Fori(1, n - 1) as i:
                body(i, False, False)
            body(n - 1, False, True)

        def mixer_stored(eng, l):
            eng.wait_ge(prow_out, START + 32 * (l + 1))
            eng.wait_ge(sp_out, START + 32 * (l + 1))
            for k in range(2):
                eng.wait_ge(so_out[k], 2 * 2 * 32 * (l + 1))

        HALVES = [(p, half) for p in range(2) for half in range(2)]

        def next_stage(eng, l, u, split, parts):
            def all_of(l2):
                for p, half in parts:
                    split(l2, u, p, half, KD)
            if u == U_F1I:
                with eng.If(l < g.L - 1):
                    all_of(l + 1)
            else:
                all_of(l)

        @block.scalar
        def _(eng):
            def hi(l, u, p, half, depth):
                n = split_size(depth)
                if half == 0:
                    eng.wait_ge(raw_landed[p], 32 * (l * PAIRS + u + 1))
                eng.wait_ge(half_used, 2 * number(l, u, p) + half + 1)
                s = slice(half * HALF, half * HALF + n)
                eng.activation(whi[p][:, s], raw[p][:, half * n:(half + 1) * n], ACT.Copy).then_inc(hi_done, 1)

            def ahead(l, u, p, depth):
                for half in range(2):
                    hi(l, u + 1, p, half, depth)

            def root(n):
                eng.wait_ge(mean_done, n)
                eng.wait_ge(r_done, START + n - 1)
                eng.activation(rb[:, :], msc[5][:, 0:T], ACT.Sqrt, bias=C("eps")).then_inc(rms_done, 1)

            def gained(l, made, m, gain):
                eng.wait_ge(x_done, START + l * X_L + made + m + 1)
                eng.activation(xh[:, m, :], x[:, m, :], ACT.Copy, scale=gl[:, bass.ds(gain * KD + m, 1)])\
                   .then_inc(xh_done, 1)

            def ffn(l, f, u_in, u_out, made, n, gain, u_next):
                def pair(i, first, last):
                    depth = KF // 2 if last else KD
                    ahead(l, u_in + i, 0, depth)
                    if first:
                        root(n)
                    for t in range(2):
                        eng.wait_ge(gate_done, f * KF + 2 * i + t + 1)
                        eng.activation(fs[t][:, :], fa[t][:, :], ACT.Silu).then_inc(silu_done, 1)
                    ahead(l, u_in + i, 1, depth)
                    for t in range(2):
                        eng.wait_ge(h_done, f * KF + 2 * i + t + 1)
                        eng.activation(hh[:, 2 * i + t, :], fh[t][:, :], ACT.Copy).then_inc(hh_done, 1)

                both_ends(eng, KF // 2, pair)

                def split(i, last, parts):
                    if last:
                        next_stage(eng, l, u_next, hi, parts)
                    else:
                        for p, half in parts:
                            hi(l, u_out + i + 1, p, half, KF // 2)

                def pair_out(i, first, last):
                    split(i, last, HALVES[:-1])
                    for t in range(2):
                        gained(l, made, 2 * i + t, gain)
                    split(i, last, HALVES[-1:])

                both_ends(eng, KD // 2, pair_out)

            for s in (sp_done, sp_out, prow_out):
                eng.sem_inc(s, START)
            ni = g.K["mean_d"].stop
            eng.dma_start(kc[:, 0:ni], a["c_all"][:, 0:ni]).then_inc(ident_in, 16)
            eng.dma_start(vrow[0:NVEC * KD, :], a["c_gains"]).then_inc(vec_in, 16)
            eng.wait_ge(ident_in, 16)
            eng.activation(identr[:, :], C("ident"), ACT.Copy).then_inc(exact_done, 1)
            eng.activation(meanr[:, :], C("mean_d"), ACT.Copy, scale=g.D / g.DV).then_inc(exact_done, 1)
            eng.wait_ge(vec_done, 1)
            for m in range(KD):
                eng.wait_ge(x_start, m + 1)
                eng.activation(xh[:, m, :], x[:, m, :], ACT.Copy, scale=vecT[:, m:m + 1]).then_inc(xh_done, 1)
                if m >= KD - 5 and m < KD - 1:
                    hi(0, 0, *HALVES[m - KD + 5], KD)
                if m == KD - 5:
                    eng.dma_start(kc[:, ni:g.NK], a["c_all"][:, ni:g.NK]).then_inc(const_in, 16)
            for l in range(g.L):
                eng.dma_start(o["state_pool_sample"][l, :, 0:BUF - NS, :], a["state_pool"][l, :, NS:BUF, :])\
                   .then_inc(old_rows, 16)

            with eng.Fori(0, g.L) as l:
                eng.wait_ge(gl_done, l + 1)
                ffn(l, 2 * l, U_F1I, U_F1O, 0, 3 * l + 1, 1, U_U)

                eng.wait_ge(ml_done, START + KD * l)
                eng.dma_start(hist, a["state_pool"][l].rearrange("b r c -> (b r) c")).then_inc(hist_in, 16)
                for p in range(2):
                    ahead(l, U_U, p, KD)
                    if p == 0:
                        root(3 * l + 2)
                    else:
                        eng.wait_ge(hist_turned, l + 1)
                        for n in range(NG):
                            eng.activation(samples(ext[:, n, :])[:, :, 0:BUF],
                                           msc[6][:, n * NB * BUF:(n + 1) * NB * BUF].rearrange("p (b r) -> p b r", r=BUF),
                                           ACT.Copy).then_inc(hist_done, 1)
                    for n in range(2 * p, 2 * p + 2):
                        eng.wait_ge(zu_done, NG * l + n + 1)
                        eng.activation(ext[:, n, BUF:g.PSEG], zu[:, n, 0:SEQ], ACT.Copy).then_inc(ext_done, 1)
                        eng.activation(samples(ext[:, n, :])[:, :, BUF:g.SEG],
                                       zu[:, n, SEQ:T].rearrange("p (b s) -> p b s", s=NS), ACT.Copy).then_inc(ext_done, 1)

                with eng.Fori(0, 2) as i:
                    half_no = 2 * l + i
                    Q4 = 4 * half_no
                    def pool_out(t, bank):
                        eng.wait_ge(pool_done, Q4 + t + 1)
                        if t == 0:
                            eng.wait_ge(gated_b, START + Q4)
                        eng.activation(pq[:, t, :], bank[:, 0:T], ACT.Copy, scale=gl[:, bass.ds(3 * KD + 4 * i + t, 1)])\
                           .then_inc(pq_done, 1)

                    def v_out(h, bank):
                        eng.wait_ge(v_turned, Q4 + h + 1)
                        eng.activation(vt[:, :, h, :], bank[:, 0:SEQ].rearrange("p (c v) -> p c v", v=P), ACT.Copy)\
                           .then_inc(vs_step, 1)
                        eng.activation(vs[0:TS, h, :], bank[0:TS, SEQ:SEQ + P], ACT.Copy).then_inc(vs_step, 1)
                        eng.activation(vs[2 * TS:3 * TS, h, :], bank[0:TS, SEQ:SEQ + P], ACT.Copy).then_inc(vt_done, 1)

                    def sigmoid_g(h):
                        eng.wait_ge(z_done, START + 5 * Q4 + 2 + 8 + h + 1)
                        eng.wait_ge(merged, START + Q4)
                        eng.activation(sg[:, h, :], z[:, h, :], ACT.Sigmoid).then_inc(sig_done, 1)

                    def sigmoid(n):
                        eng.wait_ge(z_done, START + 5 * Q4 + 2 + n + 1)
                        eng.activation(z[:, n % 4, :], z[:, n % 4, :], ACT.Sigmoid).then_inc(sig_done, 1)

                    def o_out(h, bank):
                        eng.wait_ge(o_done, Q4 + h + 1)
                        if h == 0:
                            eng.wait_ge(ml_done, START + Q4)
                        if h == 0:
                            eng.wait_ge(d_done, NG * (l + 1))
                        eng.activation(oh[:, h, :], bank[:, 0:T], ACT.Copy).then_inc(oh_done, 1)
                        if h >= 2:
                            eng.wait_ge(omean_done, Q4 + h - 1)
                        eng.activation(osq[h % 2][:, :], bank[:, 0:T], ACT.Square).then_inc(osq_done, 1)
                        eng.wait_ge(osq_done, Q4 + h + 1)
                        eng.activation(osh[h % 2][:, :], osq[h % 2][:, :], ACT.Copy).then_inc(osh_done, 1)

                    def o_root(h, bank):
                        eng.wait_ge(omean_done, Q4 + h + 1)
                        if h >= 2:
                            eng.wait_ge(normed, Q4 + h - 1)
                        eng.activation(rin[h % 2][:, :], bank[:, 0:T], ACT.Sqrt, bias=C("eps")).then_inc(orms_done, 1)

                    def swapped(t, bank):
                        if t == 0:
                            eng.wait_ge(prow_out, START + 32 * l)
                            eng.wait_ge(gated_b, START + Q4)
                        r = g.DK // 2
                        for b in range(P // r):
                            to = b ^ 1
                            ins = eng.activation(z[to * r:(to + 1) * r, t, :], bank[b * r:(b + 1) * r, 0:T], ACT.Copy)
                            ins.then_inc(swap_done, 1)

                    def upper(h):
                        eng.wait_ge(merged, START + Q4 + h + 1)
                        eng.activation(mh[:, 4 * i + h, :], oh[:, h, :], ACT.Copy).then_inc(mh_done, 1)

                    for n in range(10):
                        p, u = n % 2, U_Q + 5 * i + n // 2
                        hi(l, u + 1, p, 0, KD)
                        if n == 9:
                            for h in range(2):
                                upper(h)
                        if n < 2:
                            eng.wait_ge(half_used, done(l, u, p))
                            for t in range(2):
                                swapped(2 * n + t, big[2 * p + t])
                        if n == 9:
                            for t in (18, 19):
                                sigmoid(t)
                            for h in range(2, 4):
                                upper(h)
                        hi(l, u + 1, p, 1, KD)
                        if n == 2:
                            for t in range(4):
                                pool_out(t, msc[4 + (t + 2) % 4])
                        if n == 3:
                            for h in range(2):
                                v_out(h, msc[6 + h])
                        if n == 4:
                            for h in range(2, 4):
                                v_out(h, msc[4 + h])
                            for h in range(2):
                                sigmoid_g(h)
                        if n == 5:
                            for t in range(2):
                                eng.wait_ge(kt_done, 2 * half_no + t + 1)
                                for h in range(2 * t, 2 * t + 2):
                                    src = msc[6 + t][0:TS, SEQ + (h % 2) * g.DK:SEQ + (h % 2 + 1) * g.DK]
                                    for r in range(2):
                                        ins = eng.activation(ks[r * TS:(r + 1) * TS, h, :], src, ACT.Copy,
                                                             scale=Q("wks")[0:TS, h:h + 1])
                                        ins.then_inc(ks_done if h % 2 and r else khi_step, 1)
                            for h in range(2):
                                o_out(h, msc[4 + h])
                            for h in range(2, 4):
                                sigmoid_g(h)
                        if n == 6:
                            for t in (12, 13):
                                sigmoid(t)
                            for h in range(2, 4):
                                o_out(h, msc[4 + h])
                            for h in range(2):
                                o_root(h, msc[4 + h])
                        if n == 7:
                            for h in range(2, 4):
                                o_root(h, msc[2 + h])
                            for t in (14, 15):
                                sigmoid(t)
                        if n == 8:
                            for t in (16, 17):
                                sigmoid(t)
                            eng.wait_ge(pnew_done, half_no + 1)
                            eng.wait_ge(sp_out, START + 16 * half_no)
                            eng.activation(sp[:, :, :], msc[4][0:g.DK, :].rearrange("p (h v) -> p h v", v=P), ACT.Copy)\
                               .then_inc(sp_done, 1)
                            eng.wait_ge(sp_done, START + half_no + 1)
                            eng.dma_start(o["state_ret_prompt"][l, 0, bass.ds(QH * i, QH)].rearrange("h k v -> k h v"),
                                          sp[:, :, :]).then_inc(sp_out, 16)

                for s in range(KD // 2):
                    hi(l, U_WO + s // 2 + 1, s % 2, 0, KD)
                    for m in range(2 * s, 2 * s + 2):
                        gained(l, KD, m, 2)
                    hi(l, U_WO + s // 2 + 1, s % 2, 1, KD)
                    if s == 0:
                        eng.wait_ge(prow_turned, l + 1)
                        eng.activation(prow, msc[4][:, 0:g.PIN], ACT.Copy).then_inc(prow_done, 1)
                        eng.wait_ge(prow_done, l + 1)
                        eng.dma_start(o["state_pool_prompt"][l, 0], prow[PR:PR + BUF, :]).then_inc(prow_out, 16)
                        eng.dma_start(o["state_pool_sample"][l, :, BUF - NS:BUF, :], prow[PR + BUF:P, :]).then_inc(prow_out, 16)

                mixer_stored(eng, l)
                ffn(l, 2 * l + 1, U_F2I, U_F2O, 2 * KD, 3 * l + 3, 4, U_F1I)

            eng.wait_ge(mean_done, 3 * g.L + 1)
            eng.activation(rcol[:, :], msc[5][:, 0:len(ROWS)], ACT.Sqrt, bias=C("eps")).then_inc(rms_done, 1)
            eng.wait_ge(r_done, START + 3 * g.L + 1)
            eng.wait_ge(y_turned, KD)
            for c, _ in ROWS:
                eng.activation(tok[:, c, 0:g.D // 2], ybank[2 * c][:, :], ACT.Copy, scale=rcol[:, c:c + 1])\
                   .then_inc(y_evac[0], 1)

        @block.vector
        def _(eng):
            def lo(l, u, p, half, depth):
                n = split_size(depth)
                eng.wait_ge(hi_done, 2 * number(l, u, p) + half + 1)
                s = slice(half * HALF, half * HALF + n)
                eng.tensor_tensor(wlo[p][:, s], raw[p][:, half * n:(half + 1) * n], whi[p][:, s].bitcast(F32), ALU.subtract).then_inc(lo_done, 1)

            def ahead(l, u, p, half, depth):
                lo(l, u + 1, p, half, depth)

            def invert(n):
                eng.wait_ge(rms_done, n)
                eng.reciprocal(rb[:, :], rb[:, :]).then_inc(r_done, 1)

            def lower_x(l, made, m, gain):
                eng.wait_ge(xh_done, l * X_L + KD + made + m + 1)
                eng.scalar_tensor_tensor(xl[:, m, :], x[:, m, :], gl[:, bass.ds(gain * KD + m, 1)],
                                         xh[:, m, :].bitcast(F32), ALU.mult, ALU.subtract).then_inc(xl_done, 1)

            def ffn(l, f, u_in, u_out, made, n, gain, u_next):
                def lower_h(j, p):
                    eng.wait_ge(hh_done, f * KF + j + 1)
                    eng.tensor_tensor(hl[:, j, :], fh[p][:, :], hh[:, j, :].bitcast(F32), ALU.subtract).then_inc(hl_done, 1)

                def pair(i, first, last):
                    depth = KF // 2 if last else KD
                    ahead(l, u_in + i, 0, 0, depth)
                    if first:
                        ahead(l, u_in + i, 0, 1, depth)
                        invert(n)
                        eng.wait_ge(r_done, START + n)
                    else:
                        for t in range(2):
                            lower_h(2 * i - 2 + t, t)
                    eng.wait_ge(half_used, done(l, u_in + i, 0))
                    for t in range(2):
                        eng.tensor_tensor(fa[t][:, :], big[t][:, 0:T], rb[:, :], ALU.mult).then_inc(gate_done, 1)
                    if not first:
                        ahead(l, u_in + i, 0, 1, depth)
                    ahead(l, u_in + i, 1, 0, depth)
                    eng.wait_ge(half_used, done(l, u_in + i, 1))
                    for t in range(2):
                        eng.wait_ge(scaled_done, f * KF + 2 * i + t + 1)
                        eng.tensor_tensor(fh[t][:, :], big[2 + t][:, 0:T], fs[t][:, :], ALU.mult).then_inc(h_done, 1)
                    ahead(l, u_in + i, 1, 1, depth)

                both_ends(eng, KF // 2, pair)
                for t in range(2):
                    lower_h(KF - 2 + t, t)

                def split(i, last, parts):
                    if last:
                        next_stage(eng, l, u_next, lo, parts)
                    else:
                        for p, half in parts:
                            lo(l, u_out + i + 1, p, half, KF // 2)

                def pair_out(i, b, last):
                    split(i, last, HALVES[:-1])
                    eng.wait_ge(half_used, done(l, u_out + i, 1))
                    for t in range(2):
                        m = 2 * i + t
                        eng.scalar_tensor_tensor(x[:, m, :], big[2 * b + t][:, 0:T], 0.5, x[:, m, :], ALU.mult, ALU.add)\
                           .then_inc(x_done, 1)
                    for t in range(2):
                        lower_x(l, made, 2 * i + t, gain)
                    split(i, last, HALVES[-1:])

                with eng.Fori(0, KD // 4 - 1) as e:
                    for b in range(2):
                        pair_out(2 * e + b, b, False)
                pair_out(KD // 2 - 2, 0, False)
                pair_out(KD // 2 - 1, 1, True)

            eng.sem_inc(lo_done, 4)
            eng.sem_inc(z_done, START + 2)
            for s in (x_done, r_done, so_done, ml_done, gated_b, merged):
                eng.sem_inc(s, START)
            eng.wait_ge(vec_turned, 1)
            eng.tensor_copy(vecT[:, :], msc[7][:, 0:NVEC * KD]).then_inc(vec_done, 1)
            eng.wait_ge(vec_done, 1)
            for m in range(KD + 1):
                if m < KD:
                    eng.wait_ge(x_turned, m + 1)
                    eng.tensor_copy(x[:, m, :], big[m % 4][:, 0:T]).then_inc(x_start, 1)
                if m >= 1:
                    eng.wait_ge(xh_done, m)
                    eng.scalar_tensor_tensor(xl[:, m - 1, :], x[:, m - 1, :], vecT[:, m - 1:m], xh[:, m - 1, :].bitcast(F32),
                                             ALU.mult, ALU.subtract).then_inc(xl_done, 1)
                if m >= KD - 4 and m < KD:
                    lo(0, 0, *HALVES[m - KD + 4], KD)

            with eng.Fori(0, g.L) as l:
                eng.wait_ge(xl_done, l * X_L + KD)
                eng.tensor_copy(gl[:, :], vecT[:, bass.ds(l * 4 * KD, 5 * KD)]).then_inc(gl_done, 1)
                eng.wait_ge(gl_done, l + 1)
                ffn(l, 2 * l, U_F1I, U_F1O, 0, 3 * l + 1, 1, U_U)

                for p in range(2):
                    ahead(l, U_U, p, 0, KD)
                    if p == 0:
                        ahead(l, U_U, p, 1, KD)
                        invert(3 * l + 2)
                        eng.wait_ge(r_done, START + 3 * l + 2)
                    eng.wait_ge(half_used, done(l, U_U, p))
                    for t in range(2):
                        eng.tensor_tensor(zu[:, 2 * p + t, :], big[2 * p + t][:, 0:T], rb[:, :], ALU.mult)\
                           .then_inc(zu_done, 1)
                    if p == 1:
                        ahead(l, U_U, p, 1, KD)

                with eng.Fori(0, 2) as i:
                    half_no = 2 * l + i
                    Q4 = 4 * half_no

                    def mask(name, h, n):
                        s = g.Q[name].start + h * n
                        return qc[:, s:s + n]

                    def rotate_parts(t, bank):
                        eng.wait_ge(swap_done, 4 * (Q4 + t + 1))
                        eng.tensor_tensor(rot[:, t, :], bank[:, 0:T], C("cos"), ALU.mult).then_inc(z_done, 1)
                        eng.tensor_tensor(z[:, t, :], z[:, t, :], C("sin"), ALU.mult).then_inc(sin_done, 1)

                    def rotate_sum(t):
                        eng.wait_ge(z_done, START + 5 * Q4 + 2 + t + 1)
                        eng.wait_ge(sin_done, Q4 + t + 1)
                        eng.tensor_tensor(rot[:, t, :], rot[:, t, :], z[:, t, :], ALU.add).then_inc(rsum_done, 1)

                    def rotate_scale(t):
                        eng.wait_ge(rsum_done, Q4 + t + 1)
                        eng.scalar_tensor_tensor(rot[:, t, :], rot[:, t, :], 1.0 if t < 2 else g.DK ** -0.5, rb[:, :],
                                                 ALU.mult, ALU.mult).then_inc(rot_done, 1)

                    def decayed(h, bank):
                        eng.wait_ge(scores_done, Q4 + h + 1)
                        m = mask("mask", h, SEQ)
                        eng.tensor_tensor(sc[h][:, 0:SEQ], bank[:, 0:SEQ], m, ALU.mult).then_inc(sc_step, 1)
                        eng.tensor_tensor(sc[h][:, SEQ:SEQ + P], bank[:, SEQ:SEQ + P], m[:, 0:P], ALU.mult).then_inc(sc_step, 1)
                        for r in range(2):
                            eng.tensor_tensor(scs[h][r * TS:(r + 1) * TS, :], bank[0:TS, SEQ + P:SEQ + P + TS],
                                              mask("smask", h, TS)[0:TS, :], ALU.mult).then_inc(sc_step, 1)
                        eng.tensor_tensor(q2[h][:, :], bank[:, SEQ + P + TS:SEQ + P + 2 * TS], mask("qmask", h, TS),
                                          ALU.mult).then_inc(scores_evac, 1)

                    def k_out(t, bank):
                        eng.wait_ge(k_turned, 2 * half_no + t + 1)
                        wk = Q("wk").rearrange("p (c h) -> p c h", h=QH)[:, :, 2 * t:2 * t + 2]
                        for c in range(g.CH):
                            ins = eng.tensor_tensor(
                                kt[:, c, 2 * t:2 * t + 2, :],
                                bank[:, c * P:(c + 1) * P].rearrange("p (h k) -> p h k", k=g.DK),
                                wk[:, c, :].unsqueeze(2).to_broadcast([P, 2, g.DK]), ALU.mult)
                            ins.then_inc(kt_done if c == g.CH - 1 else kt_step, 1)

                    def v_lower(h, bank):
                        eng.wait_ge(vt_done, Q4 + h + 1)
                        eng.tensor_tensor(vs[TS:2 * TS, h, :], bank[0:TS, SEQ:SEQ + P], vs[0:TS, h, :].bitcast(F32),
                                          ALU.subtract).then_inc(vlo_done, 1)

                    def k_lower(t, bank):
                        eng.wait_ge(ks_done, 2 * half_no + t + 1)
                        for h in range(2 * t, 2 * t + 2):
                            src = bank[0:TS, SEQ + (h % 2) * g.DK:SEQ + (h % 2 + 1) * g.DK]
                            ins = eng.scalar_tensor_tensor(ks[2 * TS:3 * TS, h, :], src, Q("wks")[0:TS, h:h + 1],
                                                           ks[0:TS, h, :].bitcast(F32), ALU.mult, ALU.subtract)
                            ins.then_inc(klo_done if h % 2 else klo_step, 1)

                    def squares_lower(h):
                        eng.wait_ge(osh_done, Q4 + h + 1)
                        eng.tensor_tensor(osl[h % 2][:, :], osq[h % 2][:, :], osh[h % 2][:, :].bitcast(F32),
                                          ALU.subtract).then_inc(osl_done, 1)

                    def invert_o(h):
                        eng.wait_ge(orms_done, Q4 + h + 1)
                        eng.reciprocal(rin[h % 2][:, :], rin[h % 2][:, :]).then_inc(rin_done, 1)

                    def new_state(h, bank):
                        eng.wait_ge(snew_done, START + Q4 + h + 1)
                        eng.wait_ge(so_free, START + Q4 + h - 1)
                        eng.scalar_tensor_tensor(so[h % 2][:, :, :], st[:, :, h, :], mask("decay", h, 1),
                                                 bank[:, :].rearrange("p (b v) -> p b v", v=P), ALU.mult, ALU.add)\
                           .then_inc(so_done, 1)

                    def merge(h0, h1):
                        for h in range(h0, h1):
                            eng.wait_ge(sig_done, 12 * half_no + 8 + h + 1)
                            eng.wait_ge(pq_done, Q4 + h + 1)
                            eng.tensor_tensor(sg[:, h, :], pq[:, h, :], z[:, h, :], ALU.mult).then_inc(gated_b, 1)
                        for h in range(h0, h1):
                            eng.wait_ge(gated_b, START + Q4 + h + 1)
                            eng.wait_ge(gated_a, Q4 + h + 1)
                            eng.tensor_tensor(oh[:, h, :], oh[:, h, :], sg[:, h, :], ALU.add).then_inc(merged, 1)

                    def lower(h):
                        eng.wait_ge(mh_done, Q4 + h + 1)
                        eng.tensor_tensor(ml[:, 4 * i + h, :], oh[:, h, :], mh[:, 4 * i + h, :].bitcast(F32), ALU.subtract)\
                           .then_inc(ml_done, 1)

                    def ring_free(n):
                        if n < 8:
                            eng.wait_ge(rot_done, Q4 + n - 3)
                        elif n < 12:
                            eng.wait_ge(v_turned, Q4 + n - 7)
                        elif n < 16:
                            eng.wait_ge(sg_done, Q4 + n - 11)
                        else:
                            eng.wait_ge(gated_a, Q4 + n - 15)

                    for n in range(10):
                        p, u = n % 2, U_Q + 5 * i + n // 2
                        ahead(l, u, p, 0, KD)
                        eng.wait_ge(half_used, done(l, u, p))
                        if n < 2:
                            for t in range(2):
                                rotate_parts(2 * n + t, big[2 * p + t])
                            for t in range(2):
                                rotate_sum(2 * n + t)
                            for t in range(2):
                                rotate_scale(2 * n + t)
                            ahead(l, u, p, 1, KD)
                        else:
                            for t in range(2):
                                ring_free(2 * n + t)
                                eng.tensor_tensor(z[:, (2 * n + t) % 4, :], big[2 * p + t][:, 0:T], rb[:, :], ALU.mult)\
                                   .then_inc(z_done, 1)
                            if n == 9:
                                for h in range(2):
                                    lower(h)
                                merge(2, 4)
                                for h in range(2, 4):
                                    lower(h)
                            ahead(l, u, p, 1, KD)
                        if n == 3:
                            eng.wait_ge(half_in, HALF_IN * (half_no + 1))
                            for h in range(2):
                                decayed(h, msc[4 + h])
                            for h in range(2):
                                v_lower(h, msc[6 + h])
                        if n == 4:
                            for h in range(2, 4):
                                decayed(h, msc[2 + h])
                            for h in range(2, 4):
                                v_lower(h, msc[4 + h])
                        if n == 5:
                            for t in range(2):
                                k_out(t, msc[6 + t])
                            for t in range(2):
                                k_lower(t, msc[6 + t])
                            for h in range(2):
                                squares_lower(h)
                        if n == 6:
                            for h in range(2, 4):
                                squares_lower(h)
                            for h in range(2):
                                invert_o(h)
                        if n == 7:
                            for h in range(2):
                                new_state(h, msc[6 + h])
                            for h in range(2, 4):
                                invert_o(h)
                        if n == 8:
                            merge(0, 2)
                        if n == 9:
                            for h in range(2, 4):
                                new_state(h, msc[4 + h])

                for s in range(KD // 2):
                    u, p = U_WO + s // 2, s % 2
                    ahead(l, u, p, 0, KD)
                    eng.wait_ge(half_used, done(l, u, p))
                    for t in range(2):
                        eng.tensor_tensor(x[:, 2 * s + t, :], big[2 * p + t][:, 0:T], x[:, 2 * s + t, :], ALU.add)\
                           .then_inc(x_done, 1)
                    for t in range(2):
                        lower_x(l, KD, 2 * s + t, 2)
                    ahead(l, u, p, 1, KD)

                mixer_stored(eng, l)
                ffn(l, 2 * l + 1, U_F2I, U_F2O, 2 * KD, 3 * l + 3, 4, U_F1I)

            eng.wait_ge(rms_done, 3 * g.L + 1)
            eng.reciprocal(rcol[:, :], rcol[:, :]).then_inc(r_done, 1)
            eng.wait_ge(r_done, START + 3 * g.L + 1)
            eng.wait_ge(y_turned, KD)
            for c, _ in ROWS:
                eng.tensor_scalar(tok[:, c, g.D // 2:g.D], ybank[2 * c + 1][:, :], rcol[:, c:c + 1], None, ALU.mult)\
                   .then_inc(y_evac[1], 1)

        @block.gpsimd
        def _(eng):
            def squares(n, m, s, value):
                eng.wait_ge(s, value)
                eng.wait_ge(ssq_done, 9 * n + m + 1)
                eng.tensor_tensor(sqt[:, :], x[:, m, :], x[:, m, :], ALU.mult).then_inc(sq_done, 1)
                eng.wait_ge(sq_done, KD * n + m + 1)
                eng.tensor_tensor(ssq[:, :], ssq[:, :], sqt[:, :], ALU.add).then_inc(ssq_done, 1)

            def clear(n):
                eng.wait_ge(mean_done, n)
                eng.tensor_tensor(ssq[:, :], C("cos"), C("cos"), ALU.subtract).then_inc(ssq_done, 1)

            eng.sem_inc(so_free, START)
            eng.memset(ssq[:, :], 0.0).then_inc(ssq_done, 1)
            for m in range(KD):
                squares(0, m, x_start, m + 1)
            eng.wait_ge(const_in, 16)

            def scale(l, f):
                def pair(i):
                    for t in range(2):
                        eng.wait_ge(silu_done, f * KF + 2 * i + t + 1)
                        eng.tensor_tensor(fs[t][:, :], fs[t][:, :], rb[:, :], ALU.mult).then_inc(scaled_done, 1)
                with eng.Fori(0, KF // 2) as i:
                    pair(i)

            with eng.Fori(0, g.L) as l:
                scale(l, 2 * l)
                clear(3 * l + 1)
                with eng.Fori(0, KD) as m:
                    squares(3 * l + 1, m, x_done, START + l * X_L + m + 1)

                eng.wait_ge(hist_done, NG * (l + 1))
                zero = C("cos")[:, 0:NG * BUF].rearrange("p (n r) -> p n r", r=BUF)
                eng.tensor_tensor(ext[:, :, 0:BUF], zero, zero, ALU.subtract).then_inc(w_step, 1)
                steps = 1
                for n in range(NG):
                    eng.wait_ge(ext_done, 2 * (NG * l + n + 1))
                    src, w = ext[:, n, :], 1
                    for k in range(n + 1):
                        eng.wait_ge(w_step, W_STEPS * l + steps)
                        dst, e = win[k % 2], 2 * w - 1
                        eng.tensor_tensor(dst[:, e:g.EXT], src[:, e:g.EXT], src[:, e - w:g.EXT - w], ALU.add)\
                           .then_inc(w_step, 1)
                        steps += 1
                        src, w = dst, 2 * w
                    eng.wait_ge(w_step, W_STEPS * l + steps)
                    inv = C("inv")[:, n * 16:(n + 1) * 16]
                    eng.tensor_tensor(dp[:, n, 0:16], src[:, BUF:BUF + 16], inv, ALU.mult).then_inc(w_step, 1)
                    eng.tensor_scalar(dp[:, n, 16:SEQ], src[:, BUF + 16:g.PSEG], 1.0 / w, None, ALU.mult).then_inc(w_step, 1)
                    eng.tensor_scalar(dp[:, n, SEQ:T].rearrange("p (b s) -> p b s", s=NS),
                                      samples(src)[:, :, BUF:g.SEG], 1.0 / w, None, ALU.mult).then_inc(w_step, 1)
                    steps += 3
                    eng.wait_ge(w_step, W_STEPS * l + steps)
                    eng.tensor_tensor(dp[:, n, :], dp[:, n, :], zu[:, n, :], ALU.subtract).then_inc(d_done, 1)
                assert steps == W_STEPS

                with eng.Fori(0, 2) as i:
                    half_no = 2 * l + i
                    Q4 = 4 * half_no

                    def gated(h):
                        eng.wait_ge(sig_done, 12 * half_no + h + 1)
                        eng.tensor_tensor(sg[:, h, :], z[:, h, :], sg[:, h, :], ALU.mult).then_inc(sg_done, 1)

                    def k_masked(h):
                        eng.wait_ge(klo_done, 2 * half_no + h // 2 + 1)
                        if h >= 2:
                            eng.wait_ge(snew_done, START + Q4 + h - 1)
                        shape = [3 * TS, NB, g.DK]
                        eng.tensor_tensor(ksm[h % 2][:, :, :], ks[:, h, :].bitcast(F32).unsqueeze(1).to_broadcast(shape),
                                          Q("seq")[0:3 * TS, :].unsqueeze(2).to_broadcast(shape), ALU.mult)\
                           .then_inc(ksm_done, 1)

                    def through_gates(h):
                        eng.wait_ge(rin_done, Q4 + h + 1)
                        eng.wait_ge(oh_done, Q4 + h + 1)
                        eng.tensor_tensor(oh[:, h, :], oh[:, h, :], rin[h % 2][:, :], ALU.mult).then_inc(normed, 1)
                        eng.wait_ge(normed, Q4 + h + 1)
                        eng.tensor_tensor(oh[:, h, :], oh[:, h, :], sg[:, h, :], ALU.mult).then_inc(gated_g, 1)
                        eng.wait_ge(gated_g, Q4 + h + 1)
                        eng.wait_ge(sig_done, 12 * half_no + 4 + h + 1)
                        eng.tensor_tensor(oh[:, h, :], oh[:, h, :], z[:, h, :], ALU.mult).then_inc(gated_a, 1)

                    def state_store(h):
                        eng.wait_ge(so_done, START + Q4 + h + 1)
                        for b2 in range(2):
                            eng.dma_start(o["state_ret_sample"][l].rearrange("(b two) h k v -> two k h b v", two=2)
                                          [b2, :, 4 * i + h], so[h % 2][b2 * g.DK:(b2 + 1) * g.DK, :, :])\
                               .then_inc(so_out[h % 2], 16)

                    def state_stored(h):
                        eng.wait_ge(so_out[h % 2], 32 * (2 * half_no + h // 2 + 1))
                        eng.sem_inc(so_free, 1)

                    for h in range(4):
                        gated(h)
                    eng.wait_ge(half_in, HALF_IN * (half_no + 1))
                    for h in range(2):
                        k_masked(h)
                    for h in range(2):
                        through_gates(h)
                    for h in range(2, 4):
                        k_masked(h)
                    for h in range(2):
                        state_store(h)
                    for h in range(2, 4):
                        through_gates(h)
                    for h in range(2):
                        state_stored(h)
                    for h in range(2, 4):
                        state_store(h)
                    for h in range(2, 4):
                        state_stored(h)

                for n, made in ((3 * l + 2, KD), (3 * l + 3, 2 * KD)):
                    if made == 2 * KD:
                        scale(l, 2 * l + 1)
                    clear(n)
                    with eng.Fori(0, KD) as m:
                        squares(n, m, x_done, START + l * X_L + made + m + 1)


def _constants(g):
    import numpy as np

    f = np.float32
    PAST_LEN, ROPE_BASE, EPS = 2048, 10000.0, 1e-6
    POOL_WINDOWS = (2, 4, 8, 16)
    kc = np.zeros((P, g.NK), f)

    def put(name, table):
        kc[:, g.K[name]] = table

    put("ident", np.eye(P))
    put("mean_d", 1.0 / g.D)
    half = g.DK // 2
    row = np.arange(P)
    for par in range(2):
        put(f"dup{par}", (row[:, None] == par * g.DK + row[None, :] % g.DK).astype(f))
    pos = np.concatenate([np.arange(g.SEQ), np.tile(PAST_LEN + np.arange(g.NS), g.NB)]).astype(f)
    inv = np.power(f(ROPE_BASE), -np.linspace(0.0, 1.0, half, dtype=f)).astype(f)
    ang = (pos[None, :] * inv[row % half][:, None]).astype(f)
    sign = np.where(row % g.DK < half, -1.0, 1.0).astype(f)[:, None]
    cos, sin = np.cos(ang), np.sin(ang) * sign
    put("cos", cos)
    put("sin", sin)
    t = np.arange(16)
    put("inv", np.concatenate([1.0 / np.minimum(t + 1, w) for w in POOL_WINDOWS])[None, :])
    put("eps", EPS)

    lg = np.log1p(-np.exp2(-5.0 - np.arange(g.H, dtype=np.float64)))
    qc = np.zeros((2, P, g.NQ), f)
    j, i = np.arange(P), np.arange(g.SEQ)
    tok = np.arange(g.TS)
    b, s = tok // g.NS, tok % g.NS
    for h in range(g.H):
        half_no, hh = divmod(h, g.QH)

        def half_put(name, n, table, rows=P):
            at = g.Q[name].start + hh * n
            qc[half_no, 0:rows, at:at + n] = table

        dist = i[None, :] - j[:, None]
        half_put("mask", g.SEQ, np.where(dist >= 0, np.exp(lg[h] * np.maximum(dist, 0)), 0.0))
        dist = s[None, :] - s[:, None]
        same = b[None, :] == b[:, None]
        half_put("smask", g.TS, np.where(same & (dist >= 0), np.exp(lg[h] * np.maximum(dist, 0)), 0.0), g.TS)
        half_put("qmask", g.TS, np.where(b[None, :] % 2 == (row // g.DK)[:, None], np.exp(lg[h] * (s + 1.0))[None, :], 0.0))
        half_put("wks", 1, np.exp(lg[h] * (g.NS - 1.0 - s))[:, None], g.TS)
        half_put("decay", 1, np.exp(lg[h] * g.NS))
        for c in range(g.CH):
            qc[half_no, :, g.Q["wk"].start + c * g.QH + hh] = np.exp(lg[h] * (g.SEQ - 1.0 - (c * P + j)))
    qc[:, 0:3 * g.TS, g.Q["seq"]] = np.tile(b[:, None] == np.arange(g.NB)[None, :], (3, 1))
    return kc, qc


def kernel(**inputs):
    import numpy as np
    import concourse.bacc as bacc
    from concourse.bass_utils import run_bass_kernel_spmd

    nc = bacc.Bacc("TRN2", target_bir_lowering=False, num_devices=1)
    g = plan({n: v.shape for n, v in inputs.items()})
    kc, qc = _constants(g)
    arrays = {n: np.ascontiguousarray(inputs[n]) for n in (
        "x_prompt", "x_sample", "state_ret", "state_pool", "w_ffn1_in", "w_ffn1_out", "w_in", "w_pool", "w_out",
        "w_ffn2_in", "w_ffn2_out")}
    rows = [np.asarray(inputs[n])[l] for l in range(g.L) for n in ("norm_ffn1", "norm_mix", "norm_ffn2", "pool_scale")]
    arrays["c_gains"] = np.ascontiguousarray(np.stack(rows + [np.asarray(inputs["norm_final"])]).reshape(-1, P))
    arrays["c_all"], arrays["c_half"] = kc, qc
    outs = {
        "y_prompt": (1, g.SEQ, g.D), "y_sample": (g.NB, g.NS, g.D),
        "state_ret_prompt": (g.L, 1, g.H, g.DK, g.DV), "state_ret_sample": (g.L, g.NB, g.H, g.DK, g.DV),
        "state_pool_prompt": (g.L, 1, g.BUF, g.PIN), "state_pool_sample": (g.L, g.NB, g.BUF, g.PIN),
    }
    a = {n: nc.dram_tensor("in_" + n, v.shape, F32, kind="ExternalInput").ap() for n, v in arrays.items()}
    o = {n: nc.dram_tensor("out_" + n, s, F32, kind="ExternalOutput").ap() for n, s in outs.items()}
    decoder_step(nc, g, a, o)
    r = run_bass_kernel_spmd(nc, [{"in_" + n: v for n, v in arrays.items()}], core_ids=[0])
    return tuple(r.results[0]["out_" + n] for n in outs)
```
